# Optimizing a Trainium2 kernel written in Bass

```python
import math
import jax, jax.numpy as jnp
from jax import lax
import numpy as np

D_MODEL = 1024
BATCH = 1
SEQ = 512
DEPTH = 1

SB_HEADS = 8
SB_HEAD_DIM = 64
SB_WIDTH = SB_HEADS * SB_HEAD_DIM
SB_BLOCK = 128
GDN_HEADS = 4
GDN_HEAD_DIM = 128
GDN_WIDTH = GDN_HEADS * GDN_HEAD_DIM
GDN_CONV = 4
GDN_CHUNK = 64
D_MIX = SB_WIDTH + GDN_WIDTH
D_IN = 3 * SB_WIDTH + 4 * GDN_WIDTH + 2 * GDN_HEADS
PEER_HEADS = 8
PEER_NKEYS = 128
PEER_EXPERTS = PEER_NKEYS * PEER_NKEYS
PEER_DKEY = 256
PEER_HALF = PEER_DKEY // 2
PEER_TOPK = 16
PEER_TOKEN_BLOCK = 128
EPS = 1e-6

kernel_name = 'hybrid_stickbreak_gdn_peer'

def rms_norm(x, g):
    xf = x.astype(jnp.float32)
    y = xf * lax.rsqrt(jnp.mean(xf * xf, axis=-1, keepdims=True) + EPS)
    return (y * g.astype(jnp.float32)).astype(x.dtype)

def l2_normalize(x):
    return x * lax.rsqrt(jnp.sum(x * x, axis=-1, keepdims=True) + EPS)

def stick_breaking_attention(q, k, v):
    dtype = v.dtype
    q, k, v = (t.astype(jnp.float32) for t in (q, k, v))
    seq, head_dim = q.shape[2], q.shape[3]
    scale = head_dim ** -0.5
    outs = []
    for blk in range(seq // SB_BLOCK):
        start, end = blk * SB_BLOCK, (blk + 1) * SB_BLOCK
        z = jnp.einsum('bhqd,bhkd->bhqk', q[:, :, start:end], k[:, :, :end]) * scale
        causal = jnp.arange(end)[None, :] < (start + jnp.arange(SB_BLOCK))[:, None]
        log_keep = jnp.where(causal, jax.nn.log_sigmoid(-z), 0.0)
        rest = lax.cumsum(log_keep, axis=3, reverse=True) - log_keep
        weights = jnp.where(causal, jnp.exp(jax.nn.log_sigmoid(z) + rest), 0.0)
        outs.append(jnp.einsum('bhqk,bhkd->bhqd', weights, v[:, :, :end]))
    return jnp.concatenate(outs, axis=2).astype(dtype)

def causal_depthwise_conv(x, w):
    width, seq = w.shape[0], x.shape[1]
    xp = jnp.pad(x, ((0, 0), (width - 1, 0), (0, 0)))
    return sum(w[i] * xp[:, i:i + seq] for i in range(width))

def gated_delta_rule_chunked(q, k, v, g, beta):
    bsz, heads, seq, dk = q.shape
    dv = v.shape[-1]
    c = GDN_CHUNK
    n = seq // c
    q, k, v = (t.reshape(bsz, heads, n, c, -1) for t in (q, k, v))
    g = g.reshape(bsz, heads, n, c)
    beta = beta.reshape(bsz, heads, n, c)
    gc = lax.cumsum(g, axis=3)
    lower_incl = jnp.tril(jnp.ones((c, c), dtype=bool))
    lower_strict = jnp.tril(jnp.ones((c, c), dtype=bool), -1)
    diff = gc[..., :, None] - gc[..., None, :]
    decay_in = jnp.exp(jnp.where(lower_incl, diff, -jnp.inf))
    k_beta = k * beta[..., None]
    a_mat = jnp.where(lower_strict, jnp.einsum('bhnid,bhnjd->bhnij', k_beta, k) * decay_in, 0.0)
    eye = jnp.eye(c, dtype=q.dtype)
    t_inv = lax.linalg.triangular_solve(a_mat + eye, jnp.broadcast_to(eye, a_mat.shape),
                                        left_side=True, lower=True, unit_diagonal=True)
    u = jnp.einsum('bhnij,bhnjd->bhnid', t_inv, v * beta[..., None])
    w = jnp.einsum('bhnij,bhnjd->bhnid', t_inv, k_beta * jnp.exp(gc)[..., None])
    attn_intra = jnp.where(lower_incl, jnp.einsum('bhnid,bhnjd->bhnij', q, k) * decay_in, 0.0)
    q_dec = q * jnp.exp(gc)[..., None]
    k_dec = k * jnp.exp(gc[..., -1:] - gc)[..., None]
    chunk_decay = jnp.exp(gc[..., -1])

    def step(state, inp):
        q_c, k_c, u_c, w_c, a_c, d_c = inp
        v_new = u_c - jnp.einsum('bhcd,bhde->bhce', w_c, state)
        o_c = jnp.einsum('bhcd,bhde->bhce', q_c, state) + jnp.einsum('bhij,bhje->bhie', a_c, v_new)
        state = state * d_c[..., None, None] + jnp.einsum('bhcd,bhce->bhde', k_c, v_new)
        return state, o_c

    xs = tuple(jnp.moveaxis(t, 2, 0) for t in (q_dec, k_dec, u, w, attn_intra, chunk_decay))
    state0 = jnp.zeros((bsz, heads, dk, dv), dtype=q.dtype)
    _, o = lax.scan(step, state0, xs)
    return jnp.moveaxis(o, 0, 2).reshape(bsz, heads, seq, dv)

def gated_deltanet(qkv, z, a, b, conv_w, a_log, dt_bias, out_g):
    bsz, seq, _ = qkv.shape
    dtype = qkv.dtype
    f32 = jnp.float32
    qkv = jax.nn.silu(causal_depthwise_conv(qkv.astype(f32), conv_w.astype(f32)))
    qkv = qkv.reshape(bsz, seq, 3, GDN_HEADS, GDN_HEAD_DIM).transpose(2, 0, 3, 1, 4)
    q = l2_normalize(qkv[0]) * GDN_HEAD_DIM ** -0.5
    k = l2_normalize(qkv[1])
    v = qkv[2]
    beta = jax.nn.sigmoid(b.astype(f32)).transpose(0, 2, 1)
    g = (-jnp.exp(a_log.astype(f32)) * jax.nn.softplus(a.astype(f32) + dt_bias.astype(f32))).transpose(0, 2, 1)
    o = gated_delta_rule_chunked(q, k, v, g, beta)
    o = rms_norm(o.transpose(0, 2, 1, 3), out_g) * jax.nn.silu(
        z.astype(f32).reshape(bsz, seq, GDN_HEADS, GDN_HEAD_DIM))
    return o.reshape(bsz, seq, GDN_WIDTH).astype(dtype)

def peer_ffn(h, w_q, keys1, keys2, u_tab, v_tab):
    bsz, seq, d = h.shape
    tokens = bsz * seq
    hf = h.reshape(tokens, d)
    q = (hf @ w_q).astype(jnp.float32).reshape(tokens, PEER_HEADS, 2, PEER_HALF)
    s1 = jnp.einsum('thd,hnd->thn', q[:, :, 0], keys1.astype(jnp.float32))
    s2 = jnp.einsum('thd,hnd->thn', q[:, :, 1], keys2.astype(jnp.float32))
    v1, i1 = lax.top_k(s1, PEER_TOPK)
    v2, i2 = lax.top_k(s2, PEER_TOPK)
    cand_score = (v1[..., :, None] + v2[..., None, :]).reshape(tokens, PEER_HEADS, PEER_TOPK * PEER_TOPK)
    cand_id = (i1[..., :, None] * PEER_NKEYS + i2[..., None, :]).reshape(tokens, PEER_HEADS, PEER_TOPK * PEER_TOPK)
    top_score, pos = lax.top_k(cand_score, PEER_TOPK)
    expert_id = jnp.take_along_axis(cand_id, pos, axis=-1)
    gate = jax.nn.softmax(top_score, axis=-1)
    n_blocks = tokens // PEER_TOKEN_BLOCK
    sel = PEER_HEADS * PEER_TOPK
    xs = (hf.reshape(n_blocks, PEER_TOKEN_BLOCK, d),
          expert_id.reshape(n_blocks, PEER_TOKEN_BLOCK, sel),
          gate.reshape(n_blocks, PEER_TOKEN_BLOCK, sel))

    def block(args):
        xb, idb, gb = args
        u_sel = u_tab[idb].astype(jnp.float32)
        act = jax.nn.gelu(jnp.einsum('tkd,td->tk', u_sel, xb.astype(jnp.float32)), approximate=False)
        return jnp.einsum('tk,tkd->td', gb * act, v_tab[idb].astype(jnp.float32))

    y = lax.map(block, xs)
    return y.reshape(bsz, seq, d).astype(h.dtype)

def hybrid_layer(x, norm1_g, w_in, sb_q_norm_g, sb_k_norm_g, sb_out_norm_g, gdn_conv_w, gdn_a_log,
                 gdn_dt_bias, gdn_out_norm_g, w_out, norm2_g, peer_w_q, peer_keys1, peer_keys2,
                 peer_u, peer_v):
    bsz, seq, _ = x.shape
    h = rms_norm(x, norm1_g)
    proj = h @ w_in
    o1 = 3 * SB_WIDTH
    o2 = o1 + 3 * GDN_WIDTH
    o3 = o2 + GDN_WIDTH
    sb = proj[..., :o1].reshape(bsz, seq, 3, SB_HEADS, SB_HEAD_DIM)
    gdn_qkv = proj[..., o1:o2]
    gdn_z = proj[..., o2:o3]
    gdn_a = proj[..., o3:o3 + GDN_HEADS]
    gdn_b = proj[..., o3 + GDN_HEADS:]
    q = rms_norm(sb[:, :, 0], sb_q_norm_g).transpose(0, 2, 1, 3)
    k = rms_norm(sb[:, :, 1], sb_k_norm_g).transpose(0, 2, 1, 3)
    v = sb[:, :, 2].transpose(0, 2, 1, 3)
    sb_o = stick_breaking_attention(q, k, v).transpose(0, 2, 1, 3)
    sb_o = rms_norm(sb_o, sb_out_norm_g).reshape(bsz, seq, SB_WIDTH)
    gdn_o = gated_deltanet(gdn_qkv, gdn_z, gdn_a, gdn_b, gdn_conv_w, gdn_a_log, gdn_dt_bias, gdn_out_norm_g)
    x = x + jnp.concatenate([sb_o, gdn_o], axis=-1) @ w_out
    x = x + peer_ffn(rms_norm(x, norm2_g), peer_w_q, peer_keys1, peer_keys2, peer_u, peer_v)
    return x

def setup_inputs(seed: int = 0) -> dict:
    key = jax.random.key(seed)
    ks = jax.random.split(key, 17)
    f32 = jnp.float32
    L = DEPTH

    def nrm(k, shape, scale):
        return jax.random.normal(k, shape, f32) * scale

    def gain(k, shape):
        return 1.0 + 0.02 * jax.random.normal(k, shape, f32)

    dt = jnp.exp(jax.random.uniform(ks[8], (L, GDN_HEADS), f32, math.log(1e-3), math.log(1e-1)))
    return {
        'x': jax.random.normal(ks[0], (BATCH, SEQ, D_MODEL), f32),
        'norm1_g': gain(ks[1], (L, D_MODEL)),
        'w_in': nrm(ks[2], (L, D_MODEL, D_IN), D_MODEL ** -0.5),
        'sb_q_norm_g': gain(ks[3], (L, SB_HEAD_DIM)),
        'sb_k_norm_g': gain(ks[4], (L, SB_HEAD_DIM)),
        'sb_out_norm_g': gain(ks[5], (L, SB_HEAD_DIM)),
        'gdn_conv_w': nrm(ks[6], (L, GDN_CONV, 3 * GDN_WIDTH), GDN_CONV ** -0.5),
        'gdn_a_log': jnp.log(jax.random.uniform(ks[7], (L, GDN_HEADS), f32, 1.0, 16.0)),
        'gdn_dt_bias': dt + jnp.log(-jnp.expm1(-dt)),
        'gdn_out_norm_g': gain(ks[9], (L, GDN_HEAD_DIM)),
        'w_out': nrm(ks[10], (L, D_MIX, D_MODEL), D_MIX ** -0.5),
        'norm2_g': gain(ks[11], (L, D_MODEL)),
        'peer_w_q': nrm(ks[12], (L, D_MODEL, PEER_HEADS * PEER_DKEY), D_MODEL ** -0.5),
        'peer_keys1': nrm(ks[13], (L, PEER_HEADS, PEER_NKEYS, PEER_HALF), PEER_HALF ** -0.5),
        'peer_keys2': nrm(ks[14], (L, PEER_HEADS, PEER_NKEYS, PEER_HALF), PEER_HALF ** -0.5),
        'peer_u': nrm(ks[15], (L, PEER_EXPERTS, D_MODEL), D_MODEL ** -0.5),
        'peer_v': nrm(ks[16], (L, PEER_EXPERTS, D_MODEL), PEER_TOPK ** -0.5),
    }

def reference(x, norm1_g, w_in, sb_q_norm_g, sb_k_norm_g, sb_out_norm_g, gdn_conv_w, gdn_a_log,
              gdn_dt_bias, gdn_out_norm_g, w_out, norm2_g, peer_w_q, peer_keys1, peer_keys2,
              peer_u, peer_v):
    for layer in range(DEPTH):
        x = hybrid_layer(x, norm1_g[layer], w_in[layer], sb_q_norm_g[layer], sb_k_norm_g[layer],
                         sb_out_norm_g[layer], gdn_conv_w[layer], gdn_a_log[layer], gdn_dt_bias[layer],
                         gdn_out_norm_g[layer], w_out[layer], norm2_g[layer], peer_w_q[layer],
                         peer_keys1[layer], peer_keys2[layer], peer_u[layer], peer_v[layer])
    return x


_drawn_inputs = setup_inputs


def setup_inputs(seed=0):
    import zlib

    import numpy as np

    out = dict(_drawn_inputs(seed))
    spreads = {}
    factors = {'sb_q_norm_g': 5.552,
     'sb_k_norm_g': 6.448,
     'sb_out_norm_g': 3.399,
     'gdn_out_norm_g': 15.256,
     'norm2_g': 13.034}
    for name, (base, spread) in spreads.items():
        noise = np.random.default_rng([zlib.crc32(name.encode()), seed]).standard_normal(out[name].shape)
        drawn = base * np.exp(spread * noise) if base else spread * noise
        out[name] = __import__('jax').numpy.asarray(drawn.astype(out[name].dtype))
    for name, factor in factors.items():
        out[name] = (out[name] * factor).astype(out[name].dtype)
    return out
```

```python
import math
from contextlib import ExitStack

import concourse.bass as bass
from concourse import mybir

ALU = mybir.AluOpType
ACT = mybir.ActivationFunctionType
AX = mybir.AxisListType
F32 = mybir.dt.float32
I32 = mybir.dt.int32
U32 = mybir.dt.uint32

P = 128
D = 1024
T = 512
NT = T // P
DC = D // P
SBH, SBD = 8, 64
SBW = SBH * SBD
GH, GD = 4, 128
GW = GH * GD
CONV = 4
EPS = 1e-6
COL_GQ, COL_Z = 3 * SBW, 3 * SBW + 3 * GW
COL_AB = COL_Z + GW
PH, NKEYS, HALF, TOPK = 8, 128, 128, 16
NS = 2 * PH
SEL = PH * TOPK
NEG = -1.0e30
LOWEST = -3.0e38
LEVELS = [1 << i for i in range(7)]

KB_ORDER = [0, 1, 3, 2]
KB_OFF, _o = {}, 0
for _kb in KB_ORDER:
    KB_OFF[_kb] = _o
    _o += T - P * _kb
RAG = _o
PARTS = [(0, 512, [0]), (512, 512, [1, 3]), (1024, 256, [2])]

KB = 256

BLOCKS = ["gq", "gk", "gv", "z", "sq", "sk", "sv"]
BLOCK_COL = {"gq": COL_GQ, "gk": COL_GQ + GW, "gv": COL_GQ + 2 * GW, "z": COL_Z,
             "sq": 0, "sk": SBW, "sv": 2 * SBW}
NUNIT = 4 * len(BLOCKS)


def stage_a_order():
    steps = []
    for p in range(NUNIT):
        steps.append(("proj", p))
        if 2 <= p < 14:
            steps.append(("fwd", p - 2))
        if 8 <= p < 12:
            steps.append(("gback", p - 8))
        if 14 <= p < 18:
            steps.append(("gback", p - 10))
        if 22 <= p < 26:
            steps.append(("sback", p - 22))
    return steps + [("sback", 4 + i) for i in range(4)]


def stage_b_order():
    gdn = []
    for t in range(NT):
        gdn.append(("bc", t, 0))
        gdn.append(("kk", t, 0))
        for lv in range(len(LEVELS)):
            gdn.append(("x", t, lv))
            gdn.append(("y", t, lv))
        gdn += [("nw", t, 0), ("vn", t, 0), ("os", t, 0)]
    sb = []
    for h in range(SBH + 2):
        if h < SBH:
            sb += [("z", h, i) for i in range(3)]
        if 1 <= h <= SBH:
            sb += [("r", h - 1, i) for i in range(3)]
        if h >= 2:
            sb.append(("o", h - 2, 0))
    out, j = [], 0
    for i, g in enumerate(gdn):
        out.append(g)
        want = math.ceil(len(sb) * (i + 1) / len(gdn))
        out += sb[j:want]
        j = want
    return out


def layer_kernel(nc, x, norm1_g, w_in, sb_q_norm_g, sb_k_norm_g, sb_out_norm_g, gdn_conv_w, gdn_a_log,
                 gdn_dt_bias, gdn_out_norm_g, w_out, norm2_g, peer_w_q, keys_t, peer_u, peer_v, out):
    x_d = x[0].rearrange("(t p) d -> p t d", p=P)
    out_d = out[0].rearrange("(t p) d -> p t d", p=P)
    w_in_d = w_in[0].rearrange("(c p) n -> p c n", p=P)
    w_out_d = w_out[0].rearrange("(c p) n -> p c n", p=P)
    w_q_d = peer_w_q[0].rearrange("(c p) n -> p c n", p=P)
    u_d, v_d = peer_u[0], peer_v[0]

    with ExitStack() as ctx:
        def sb(name, shape, dt=F32):
            return ctx.enter_context(nc.sbuf_tensor(name, shape, dt))

        def sem(name):
            return ctx.enter_context(nc.semaphore(name))

        arena = sb("arena", [P, 190 * KB])

        def at(kb, *shape):
            n = math.prod(shape)
            o = int(kb * KB)
            v = arena[:, o:o + n]
            if len(shape) == 2:
                v = v.rearrange("p (a b) -> p a b", a=shape[0])
            elif len(shape) == 3:
                v = v.rearrange("p (a b c) -> p a b c", a=shape[0], b=shape[1])
            return v

        xs = at(0, NT, D)
        hT = at(16, DC, T)
        wbuf = [at(32 + 16 * i, DC, 512) for i in range(3)]
        tok = {"gq": at(80, NT, GW), "gk": at(88, NT, GW), "gv": at(96, NT, GW), "z": at(120, NT, GW),
               "sq": at(128, NT, SBW), "sk": at(136, NT, SBW), "sv": at(144, NT, SBW)}
        gqT, gkT = at(104, GH, T), at(112, GH, T)
        sqT, skT = at(152, SBH // 2, T), at(160, SBH // 2, T)
        xn = at(168, NT, D)
        raw = [at(168 + 2.25 * i, T + CONV - 1) for i in range(2)]
        conv = [at(173 + 2 * i, T) for i in range(2)]
        act_o = [at(177 + 2 * i, T) for i in range(2)]
        squares = at(182, NT * GW)
        zs = [at(16 + 5 * i, RAG) for i in range(2)]
        ez = at(26, RAG)
        sp_ = at(168, RAG)
        wts = [at(173 + 5 * i, RAG) for i in range(2)]
        w_out_s = at(32, DC, D)
        decT, qdT, kbT, AT = (at(64 + 2 * i, GH, P) for i in range(4))
        attnT, TI, ATs0, ATs1 = (at(72 + 2 * i, GH, P) for i in range(4))
        ATs = [ATs0, ATs1]
        TTI, XW, S = (at(184 + 2 * i, GH, P) for i in range(3))
        kd, vb, kbe = at(136, NT, GW), tok["gv"], tok["gk"]
        og, osb = tok["gq"], tok["sq"]
        scratch = tok["gk"]
        mixT = at(16, DC, T)
        w_q_s = at(104, DC, 2 * PH * HALF)
        h2 = at(168, NT, D)
        h2T = at(64, DC, T)
        qT = at(32, NS, T)
        keysT = at(80, NS, NKEYS)

        UB, VB = 8, 8
        u_row = [at(88 + 4 * i, D) for i in range(UB)]
        v_row = [at(120 + 4 * i, D) for i in range(VB)]
        diag = [at(184 + 0.5 * i, P) for i in range(VB)]
        qs = at(152, NS, P)
        y_s = at(160, D)
        eid = at(164, SEL).bitcast(U32)
        gates, dots, gel, wt = (at(164.5 + 0.5 * i, SEL) for i in range(4))
        top = at(16, 2, TOPK)
        topi = at(16.25, 2, TOPK).bitcast(U32)
        rest = at(17, 2, NKEYS)
        cand, crest = at(18, TOPK * TOPK), at(19, TOPK * TOPK)
        eq1, eq2 = at(20, TOPK, TOPK), at(21, TOPK, TOPK)
        best, ebest, id1, id2, nmax, esum, erec = (at(22 + i * 0.0625, TOPK) for i in range(7))
        pos, pos1, pos2 = (at(23 + i * 0.0625, TOPK).bitcast(U32) for i in range(3))

        iota = sb("iota", [P, TOPK])
        ident = sb("ident", [P, P])
        ones = sb("ones", [P, P])
        tri_ge = sb("tri_ge", [P, P])
        tri_gt = sb("tri_gt", [P, P])
        tri_le = sb("tri_le", [P, P])
        causal_add = sb("causal_add", [P, P])
        sb_mask = sb("sb_mask", [P, RAG])
        lv_mask = sb("lv_mask", [P, len(LEVELS), P])
        g1c = sb("g1c", [P, DC])
        sgc = sb("sgc", [P, 3])
        ggc = sb("ggc", [P, 1])
        cwc = sb("cwc", [P, 3 * GH, CONV])
        abc = sb("abc", [P, 2 * GH])
        g2b = sb("g2b", [P, D])
        st = sb("st", [P, 4, 32])
        ab = sb("ab", [P, NT, 2 * GH])
        gt = sb("gt", [P, 10, NT, GH])
        g_, beta, ngc, egc, nbe, ekd, etot, gt1, gt2, gt3 = (gt[:, i] for i in range(10))

        psum = ctx.enter_context(nc.psum_tensor("psum", [P, 8, 512], F32))
        bank = [psum[:, i] for i in range(8)]

        u_in = [sem(f"u_in{i}") for i in range(UB)]
        v_in = [sem(f"v_in{i}") for i in range(VB)]
        s = {n: sem(n) for n in (
            "y_out", "stored", "dve_turns", "pool_turns", "qs_rdy", "sc_ps", "best_rdy", "e_out", "eid_rdy", "u_free", "v_free",
            "h2p_rdy", "gel_rdy", "dots_rdy", "w_rdy", "diag_rdy",
            "x_in", "par_in", "w0_in", "w1_in", "w2_in", "wab_in", "wout_in", "wq_in", "keys_in",
            "consts", "xn_rdy", "xT_ps", "hT_rdy", "ab_ps", "ab_rdy",
            "proj_ps", "proj_out", "conv_done", "silu_done", "tr_ps", "tr_out", "gnorm", "snorm",
            "raw_clear", "gate_dve", "gate_act", "gate_ps", "gate_mul",
            "z_ps", "z_out", "nabs_rdy", "e_rdy", "l_rdy", "sp_rdy", "r_ps", "arg_rdy", "wt_rdy",
            "o_ps", "o_out",
            "bc_ps", "arg_g", "dec_rdy", "kb_rdy", "qd_rdy", "kk_ps", "at_rdy", "ats_rdy",
            "x_ps", "x_out", "y_ps", "ti_rdy", "nw_ps", "nw_out", "vn_ps", "vn_out", "os_ps", "os_out",
            "s_rdy", "mix_rdy", "mixT_ps", "mixT_out", "wo_ps", "x2_rdy", "ss2", "h2_rdy", "h2T_ps", "h2T_out",
            "q_ps", "q_out")}
        A_ORDER, B_ORDER = stage_a_order(), stage_b_order()
        TR = [st_ for st_ in A_ORDER if st_[0] != "proj"]

        def head_col(v, h):
            return v[:, :, h]

        h2p = psum[:, 4:6].rearrange("p a b -> p (a b)")

        def by_itself(eng, semaphore, value):
            eng.wait_ge(semaphore, value)
            eng.sem_inc(s["dve_turns" if eng is nc.vector else "pool_turns"], 1)

        def tiles(eng, body):
            with eng.Fori(0, NT - 1) as i:
                body(i, True)
            body(NT - 1, False)

        block = ctx.enter_context(nc.Block())

        @block.sync
        def _(sp):
            sp.dma_start(xs, x_d).then_inc(s["x_in"], 16)
            sp.dma_start(at(80, DC, 2 * GH), w_in_d[:, :, COL_AB:COL_AB + 2 * GH]).then_inc(s["wab_in"], 16)
            pars = [(g1c[:], norm1_g),
                    (ggc[:], gdn_out_norm_g[0].rearrange("(p o) -> p o", o=1)),
                    (abc[:, 0:GH], gdn_a_log[0].partition_broadcast(P)),
                    (abc[:, GH:2 * GH], gdn_dt_bias[0].partition_broadcast(P)),
                    (g2b[:], norm2_g[0].partition_broadcast(P))]
            for i, g in enumerate((sb_q_norm_g, sb_k_norm_g, sb_out_norm_g)):
                for half in range(2):
                    pars.append((sgc[half * SBD:(half + 1) * SBD, i:i + 1],
                                 g[0].rearrange("(p o) -> p o", o=1)))
            pars.append((cwc[:], gdn_conv_w))
            assert len(pars) == NPAR
            for dst, src in pars:
                sp.dma_start(dst, src).then_inc(s["par_in"], 16)
            for b, name in enumerate(BLOCKS):
                if b >= 3:
                    sp.wait_ge(s["proj_ps"], 4 * (b - 2))
                c0 = BLOCK_COL[name]
                sp.dma_start(wbuf[b % 3], w_in_d[:, :, c0:c0 + 512]).then_inc(s[f"w{b % 3}_in"], 16)
            sp.wait_ge(s["proj_ps"], NUNIT)
            sp.dma_start(w_out_s, w_out_d).then_inc(s["wout_in"], 16)
            sp.wait_ge(s["mixT_ps"], DC)
            sp.dma_start(w_q_s, w_q_d).then_inc(s["wq_in"], 16)
            sp.dma_start(keysT, keys_t[0].rearrange("a d n -> d a n")).then_inc(s["keys_in"], 16)
            with sp.Fori(0, NT) as i:
                sp.wait_ge(s["y_out"], i + 2)
                sp.dma_start(out_d[:, bass.ds(i, 1)].rearrange("p o d -> p (o d)"), y_s).then_inc(s["stored"], 16)
            sp.wait_ge(s["stored"], 16 * (NT + 1))

        @block.gpsimd
        def _(pool):
            pool.memset(ones[:], 1.0)
            pool.memset(sb_mask[:], 0.0)
            pool.memset(causal_add[:], 0.0)
            pool.memset(lv_mask[:], 1.0)
            pool.drain()

            def tri(dst, src, op, base, cm, step, fill):
                return pool.affine_select(out=dst, in_=src, compare_op=op, fill=fill, base=base,
                                          pattern=[[step, P]], channel_multiplier=cm)
            tri(ident[:], ones[:], ALU.is_equal, 0, 1, -1, 0.0)
            tri(tri_ge[:], ones[:], ALU.is_ge, 0, 1, -1, 0.0)
            tri(tri_gt[:], ones[:], ALU.is_gt, 0, 1, -1, 0.0)
            tri(tri_le[:], ones[:], ALU.is_ge, 0, -1, 1, 0.0)
            tri(causal_add[:], causal_add[:], ALU.is_ge, 0, -1, 1, NEG)
            for kb in range(NT):
                o = sb_mask[:, KB_OFF[kb]:KB_OFF[kb] + P]
                tri(o, o, ALU.is_gt, 0, -1, 1, NEG)
            for lv, z in enumerate(LEVELS):
                n = P // (2 * z)
                m = lv_mask[:, lv].rearrange("p (b h z) -> p b h z", b=n, h=2)
                pool.memset(m[:, :, 0], 0.0)
                pool.drain()
                pool.affine_select(out=m, in_=m, compare_op=ALU.is_ge, fill=0.0, base=0,
                                   pattern=[[-2 * z, n], [0, 2], [0, z]], channel_multiplier=1)
                pool.drain()
                last = pool.affine_select(out=m, in_=m, compare_op=ALU.is_ge, fill=0.0, base=z - 1,
                                          pattern=[[2 * z, n], [0, 2], [0, z]], channel_multiplier=-1)
            pool.iota(iota[:], pattern=[[1, TOPK]], base=0, channel_multiplier=0,
                      allow_small_or_imprecise_dtypes=True)
            pool.drain()
            pool.engine_nop().then_inc(s["consts"], 1)

            pool.wait_ge(s["gate_dve"], 4)
            pool.wait_ge(s["tr_out"], len(TR))

            def on_rows(dst, src, gate):
                for t in range(NT):
                    last = pool.tensor_tensor(
                        dst[:, t].rearrange("p (h d) -> p h d", h=GH), src[:, t].rearrange("p (h d) -> p h d", h=GH),
                        gate[:, t].unsqueeze(2).to_broadcast([P, GH, GD]), ALU.mult)
                return last
            on_rows(kd, tok["gk"], ekd)
            on_rows(vb, vb, beta)
            pool.drain()
            on_rows(kbe, kbe, nbe).then_inc(s["gate_mul"], 1)
            for t in range(NT):
                for lv in range(len(LEVELS)):
                    n = t * len(LEVELS) + lv
                    if lv == 0:
                        pool.wait_ge(s["at_rdy"], t + 1)
                    if n >= 2:
                        pool.wait_ge(s["x_ps"], n - 1)
                    pool.tensor_tensor(ATs[n % 2], AT, lv_mask[:, lv].unsqueeze(1).to_broadcast([P, GH, P]),
                                       ALU.mult).then_inc(s["ats_rdy"], 1)

            def gather(buf, table, col, landed):
                pool.indirect_dma_start(buf, None, table, bass.IndirectOffsetOnAxis(ap=eid[:, col:col + 1], axis=0)
                                        ).then_inc(landed, 16)

            def tile(i, has_next):
                for h in range(PH + 1):
                    if h < PH:
                        by_itself(pool, s["eid_rdy"], i * PH + h + 1)
                    for k in range(TOPK):
                        if h < PH:
                            c = h * TOPK + k
                            by_itself(pool, s["u_free"], i * SEL + c + 1)
                            gather(u_row[c % UB], u_d, c, u_in[c % UB])
                        if h >= 1:
                            c = (h - 1) * TOPK + k
                            by_itself(pool, s["v_free"], SEL + i * SEL + c - VB + 1)
                            gather(v_row[c % VB], v_d, c, v_in[c % VB])

            pool.wait_ge(s["q_out"], NS)
            tiles(pool, tile)

        @block.tensor
        def _(pe):
            pe.wait_ge(s["consts"], 1)
            for dc in range(DC):
                if dc == 0:
                    pe.wait_ge(s["xn_rdy"], NT)
                if dc >= 2:
                    pe.wait_ge(s["hT_rdy"], dc - 1)
                for t in range(NT):
                    mm = pe.transpose(bank[4 + dc % 2][:, t * P:(t + 1) * P], xn[:, t, dc * P:(dc + 1) * P], ident[:])
                mm.then_inc(s["xT_ps"], 1)
            pe.wait_ge(s["hT_rdy"], DC)
            pe.wait_ge(s["wab_in"], 16)
            for t in range(NT):
                for dc in range(DC):
                    mm = pe.matmul(bank[7][:, t * 2 * GH:(t + 1) * 2 * GH], hT[:, dc, t * P:(t + 1) * P],
                                   at(80, DC, 2 * GH)[:, dc], start=dc == 0, stop=dc == DC - 1)
            mm.then_inc(s["ab_ps"], 1)
            n = 0
            for kind, i in A_ORDER:
                if kind == "proj":
                    b, u = divmod(i, 4)
                    if u == 0:
                        pe.wait_ge(s[f"w{b % 3}_in"], 16 * (b // 3 + 1))
                    if i >= 4:
                        pe.wait_ge(s["proj_out"], i - 3)
                    w, ps = wbuf[b % 3], bank[i % 4]
                    for dc in range(DC):
                        if b < 3:
                            mm = pe.matmul(ps[:], w[:, dc, u * P:(u + 1) * P], hT[:, dc], start=dc == 0, stop=dc == DC - 1)
                        else:
                            mm = pe.matmul(ps[:], hT[:, dc, u * P:(u + 1) * P], w[:, dc], start=dc == 0, stop=dc == DC - 1)
                    mm.then_inc(s["proj_ps"], 1)
                    continue
                ps = bank[4 + n % 3]
                if n >= 3:
                    pe.wait_ge(s["tr_out"], n - 2)
                for t in range(NT):
                    if kind == "fwd":
                        pe.wait_ge(s["silu_done"], i + 1)
                        src = act_o[i % 2][:, t * P:(t + 1) * P]
                    elif kind == "gback":
                        pe.wait_ge(s["gnorm"], i // GH + 1)
                        src = tok["gq" if i < GH else "gk"][:, t, (i % GH) * GD:(i % GH + 1) * GD]
                    else:
                        pe.wait_ge(s["snorm"], i // 4 + 1)
                        src = tok["sq" if i < 4 else "sk"][:, t, (i % 4) * P:(i % 4 + 1) * P]
                    mm = pe.transpose(ps[:, t * P:(t + 1) * P], src, ident[:])
                mm.then_inc(s["tr_ps"], 1)
                n += 1

            pe.wait_ge(s["gate_dve"], 2)
            gall = g_.rearrange("p t h -> p (t h)")
            pe.matmul(bank[7][:, 0:16], tri_le[:], gall, start=True, stop=True)
            pe.matmul(bank[7][:, 16:32], tri_gt[:], gall, start=True, stop=True)
            pe.matmul(bank[7][:, 32:48], ones[:], gall, start=True, stop=True).then_inc(s["gate_ps"], 1)
            NL = len(LEVELS)

            def sb_part(kind, h, i):
                off, width, kbs = PARTS[i]
                n = 3 * h + i
                if kind == "z":
                    ps = bank[n % 2]
                    if h == 0 and i == 0:
                        pe.wait_ge(s["tr_out"], len(TR))
                    if n >= 2:
                        pe.wait_ge(s["z_out"], n - 1)
                    r = slice((h % 2) * SBD, (h % 2 + 1) * SBD)
                    for j, kb in enumerate(kbs):
                        o = KB_OFF[kb] - off
                        mm = pe.matmul(ps[:, o:o + T - kb * P], skT[r, h // 2, kb * P:(kb + 1) * P],
                                       sqT[r, h // 2, kb * P:T], start=True, stop=True)
                    mm.then_inc(s["z_ps"], 1)
                elif kind == "r":
                    if i == 0:
                        pe.wait_ge(s["sp_rdy"], h + 1)
                    if n >= 1:
                        pe.wait_ge(s["arg_rdy"], n)
                    ops = []
                    for kb in kbs:
                        o = KB_OFF[kb] - off
                        ops.append((tri_ge, o, KB_OFF[kb], T - kb * P))
                        for k2 in range(kb + 1, NT):
                            ops.append((ones, o + (k2 - kb) * P, KB_OFF[k2], T - k2 * P))
                    for j, (m, o, src, w) in enumerate(ops):
                        mm = pe.matmul(bank[2][:, o:o + w], m[:], sp_[:, src:src + w], start=j == 0,
                                       stop=j == len(ops) - 1, skip_group_check=True)
                    mm.then_inc(s["r_ps"], 1)
                else:
                    pe.wait_ge(s["wt_rdy"], h + 1)
                    if h >= 1:
                        pe.wait_ge(s["o_out"], h)
                    for qt in range(NT):
                        for kb in range(qt + 1):
                            o = KB_OFF[kb] + (qt - kb) * P
                            mm = pe.matmul(bank[3][:, qt * SBD:(qt + 1) * SBD], wts[h % 2][:, o:o + P],
                                           tok["sv"][:, kb, h * SBD:(h + 1) * SBD], start=kb == 0, stop=kb == qt)
                    mm.then_inc(s["o_ps"], 1)

            for kind, t, i in B_ORDER:
                n = t * NL + i
                if kind in ("z", "r", "o"):
                    sb_part(kind, t, i)
                elif kind == "bc":
                    if t == 0:
                        pe.wait_ge(s["gate_dve"], 4)
                    else:
                        pe.wait_ge(s["os_out"], t)
                        pe.wait_ge(s["s_rdy"], t + 1)
                    for h in range(GH):
                        c = slice(h * P, (h + 1) * P)
                        pe.matmul(bank[4][:, c], g_[:, t, h:h + 1].to_broadcast([P, P]), tri_le[:], start=True, stop=True)
                        mm = pe.matmul(bank[5][:, c], beta[:, t, h:h + 1].to_broadcast([P, P]), ident[:],
                                       start=True, stop=True)
                    mm.then_inc(s["bc_ps"], 1)
                elif kind == "kk":
                    pe.wait_ge(s["kb_rdy"], t + 1)
                    for h in range(GH):
                        c = slice(h * P, (h + 1) * P)
                        kt = gkT[:, h, t * P:(t + 1) * P]
                        pe.matmul(bank[6][:, c], kt, kbT[:, h], start=True, stop=True)
                        mm = pe.matmul(bank[7][:, c], kt, gqT[:, h, t * P:(t + 1) * P], start=True, stop=True)
                    mm.then_inc(s["kk_ps"], 1)
                elif kind == "x":
                    pe.wait_ge(s["ats_rdy"], n + 1)
                    if i >= 1:
                        pe.wait_ge(s["ti_rdy"], 2 * n)
                    for h in range(GH):
                        mm = pe.matmul(bank[4][:, h * P:(h + 1) * P], ATs[n % 2][:, h], TI[:, h] if i else ident[:],
                                       start=True, stop=True)
                    mm.then_inc(s["x_ps"], 1)
                elif kind == "y":
                    pe.wait_ge(s["x_out"], n + 1)
                    for h in range(GH):
                        c = slice(h * P, (h + 1) * P)
                        tt = TTI[:, h] if i else ident[:]
                        if i < NL - 1:
                            pe.matmul(bank[5][:, c], tt, XW[:, h], start=True, stop=True)
                        mm = pe.matmul(bank[6][:, c], XW[:, h], tt, start=True, stop=True)
                    mm.then_inc(s["y_ps"], 1)
                elif kind == "nw":
                    pe.wait_ge(s["ti_rdy"], 2 * (n + NL))
                    pe.wait_ge(s["gate_mul"], 1)
                    for h in range(GH):
                        mm = pe.matmul(bank[4][:, h * P:(h + 1) * P], kbe[:, t, h * GD:(h + 1) * GD], TTI[:, h],
                                       start=True, stop=True)
                    mm.then_inc(s["nw_ps"], 1)
                elif kind == "vn":
                    pe.wait_ge(s["nw_out"], t + 1)
                    pe.wait_ge(s["s_rdy"], t + 1)
                    for h in range(GH):
                        c = slice(h * P, (h + 1) * P)
                        pe.matmul(bank[5][:, c], TTI[:, h], vb[:, t, h * GD:(h + 1) * GD], start=True, stop=False)
                        mm = pe.matmul(bank[5][:, c], XW[:, h], S[:, h], start=False, stop=True)
                    mm.then_inc(s["vn_ps"], 1)
                elif kind == "os":
                    pe.wait_ge(s["vn_out"], t + 1)
                    for h in range(GH):
                        c = slice(h * P, (h + 1) * P)
                        pe.matmul(bank[6][:, c], qdT[:, h], S[:, h], start=True, stop=False)
                        pe.matmul(bank[6][:, c], attnT[:, h], kbT[:, h], start=False, stop=True)
                        mm = pe.matmul(bank[7][:, c], kd[:, t, h * GD:(h + 1) * GD], kbT[:, h], start=True, stop=True)
                    mm.then_inc(s["os_ps"], 1)

            pe.wait_ge(s["mix_rdy"], 2)
            for c in range(DC):
                if c >= 2:
                    pe.wait_ge(s["mixT_out"], c - 1)
                for t in range(NT):
                    src = osb[:, t, c * P:(c + 1) * P] if c < 4 else og[:, t, (c - 4) * P:(c - 3) * P]
                    mm = pe.transpose(bank[c % 2][:, t * P:(t + 1) * P], src, ident[:])
                mm.then_inc(s["mixT_ps"], 1)
            pe.wait_ge(s["mixT_out"], DC)
            pe.wait_ge(s["wout_in"], 16)
            for t in range(NT):
                for half in range(2):
                    n = 2 * t + half
                    if n >= 4:
                        pe.wait_ge(s["x2_rdy"], n - 3)
                    for c in range(DC):
                        mm = pe.matmul(bank[4 + n % 4][:], mixT[:, c, t * P:(t + 1) * P],
                                       w_out_s[:, c, half * 512:(half + 1) * 512], start=c == 0, stop=c == DC - 1)
                    mm.then_inc(s["wo_ps"], 1)
            for c in range(DC):
                if c == 0:
                    pe.wait_ge(s["h2_rdy"], NT)
                if c >= 2:
                    pe.wait_ge(s["h2T_out"], c - 1)
                for t in range(NT):
                    mm = pe.transpose(bank[c % 2][:, t * P:(t + 1) * P], h2[:, t, c * P:(c + 1) * P], ident[:])
                mm.then_inc(s["h2T_ps"], 1)
            pe.wait_ge(s["h2T_out"], DC)
            pe.wait_ge(s["wq_in"], 16)
            for j in range(NS):
                if j >= 4:
                    pe.wait_ge(s["q_out"], j - 3)
                for c in range(DC):
                    mm = pe.matmul(bank[j % 4][:], w_q_s[:, c, j * HALF:(j + 1) * HALF], h2T[:, c],
                                   start=c == 0, stop=c == DC - 1)
                mm.then_inc(s["q_ps"], 1)

            def scores(t):
                pe.wait_ge(s["qs_rdy"], t + 1)
                for j in range(NS):
                    mm = pe.matmul(bank[j // 4][:, (j % 4) * NKEYS:(j % 4 + 1) * NKEYS], qs[:, j], keysT[:, j],
                                   start=True, stop=True)
                mm.then_inc(s["sc_ps"], 1)

            pe.wait_ge(s["keys_in"], 16)
            scores(0)
            x2 = xs.rearrange("p t d -> p (t d)")
            pe.wait_ge(s["x2_rdy"], 2 * NT)

            def tile(i, has_next):
                pe.wait_ge(s["y_out"], i + 1)
                for half in range(2):
                    pe.matmul(bank[6 + half][:], ident[:], x2[:, bass.ds(i * D + half * 512, 512)], start=True,
                              stop=False, skip_group_check=True)
                for c in range(SEL):
                    if c == TOPK and has_next:
                        pe.wait_ge(s["eid_rdy"], i * PH + PH)
                        scores(i + 1)
                    pe.wait_ge(s["diag_rdy"], i * SEL + c + 1)
                    pe.wait_ge(v_in[c % VB], 16 * (i * (SEL // VB) + c // VB + 1))
                    for half in range(2):
                        mm = pe.matmul(bank[6 + half][:], diag[c % VB], v_row[c % VB][:, half * 512:(half + 1) * 512],
                                       start=False, stop=c == SEL - 1, skip_group_check=True)
                    mm.then_inc(s["v_free"], 1)

            tiles(pe, tile)

        @block.scalar
        def _(act):
            n = 0
            for kind, i in A_ORDER:
                if kind == "proj":
                    b, u = divmod(i, 4)
                    act.wait_ge(s["proj_ps"], i + 1)
                    if b < 3:
                        act.wait_ge(s["raw_clear"], 1)
                        if i >= 2:
                            act.wait_ge(s["conv_done"], i - 1)
                        act.copy(raw[i % 2][:, CONV - 1:], bank[i % 4][:]).then_inc(s["proj_out"], 1)
                    elif BLOCKS[b] == "z":
                        act.activation(tok["z"][:, u], bank[i % 4][:], ACT.Silu).then_inc(s["proj_out"], 1)
                    else:
                        act.copy(tok[BLOCKS[b]][:, u], bank[i % 4][:]).then_inc(s["proj_out"], 1)
                    if 1 <= i <= 12:
                        j = i - 1
                        act.wait_ge(s["conv_done"], j + 1)
                        if j >= 2:
                            act.wait_ge(s["tr_ps"], j - 1)
                        act.activation(act_o[j % 2], conv[j % 2], ACT.Silu).then_inc(s["silu_done"], 1)
                    continue
                act.wait_ge(s["tr_ps"], n + 1)
                ps = bank[4 + n % 3][:]
                if kind == "fwd":
                    if i == 0:
                        act.wait_ge(s["ab_rdy"], 1)
                    h = i % GH
                    dst = tok[BLOCKS[i // GH]][:, :, h * GD:(h + 1) * GD]
                    ins = act.copy(dst, ps.rearrange("p (t d) -> p t d", t=NT))
                elif kind == "gback":
                    ins = act.copy((gqT if i < GH else gkT)[:, i % GH], ps)
                else:
                    act.wait_ge(s["par_in"], 16 * NPAR)
                    ins = act.activation((sqT if i < 4 else skT)[:, i % 4], ps, ACT.Copy,
                                         scale=sgc[:, i // 4:i // 4 + 1])
                ins.then_inc(s["tr_out"], 1)
                n += 1

            act.activation(st[:, 3, 0:GH], abc[:, 0:GH], ACT.Exp).then_inc(s["gate_act"], 1)
            act.wait_ge(s["gate_dve"], 1)
            act.activation(gt2, gt2, ACT.Exp)
            act.activation(gt3, ab[:, :, GH:], ACT.Exp, scale=-1.0)
            act.drain()
            act.activation(gt2, gt2, ACT.Ln, bias=1.0).then_inc(s["gate_act"], 1)
            act.wait_ge(s["gate_ps"], 1)
            sums = bank[7][:, 0:48].rearrange("p (a t h) -> p a t h", a=3, t=NT)
            act.mul(ngc, sums[:, 0], -1.0)
            act.activation(egc, sums[:, 0], ACT.Exp)
            act.activation(ekd, sums[:, 1], ACT.Exp)
            act.activation(etot, sums[:, 2], ACT.Exp).then_inc(s["gate_act"], 1)

            for kind, t, i in B_ORDER:
                n = t * len(LEVELS) + i
                if kind == "z" and i == 2:
                    h = t
                    act.wait_ge(s["nabs_rdy"], h + 1)
                    act.activation(ez, ez, ACT.Exp).then_inc(s["e_rdy"], 1)
                    act.wait_ge(s["e_rdy"], h + 1)
                    act.activation(ez, ez, ACT.Ln, bias=1.0).then_inc(s["l_rdy"], 1)
                elif kind == "r" and i == 2:
                    h = t
                    act.wait_ge(s["arg_rdy"], 3 * h + 3)
                    if h >= 2:
                        act.wait_ge(s["o_ps"], h - 1)
                    act.activation(wts[h % 2], zs[h % 2], ACT.Exp).then_inc(s["wt_rdy"], 1)
                elif kind == "o":
                    h = t
                    act.wait_ge(s["o_ps"], h + 1)
                    act.copy(osb[:, :, h * SBD:(h + 1) * SBD],
                             bank[3][:, 0:NT * SBD].rearrange("p (t d) -> p t d", t=NT)).then_inc(s["o_out"], 1)
                elif kind == "bc":
                    act.wait_ge(s["bc_ps"], t + 1)
                    if t >= 1:
                        act.wait_ge(s["os_ps"], t)
                    act.activation(qdT, bank[4][:].rearrange("p (h i) -> p h i", h=GH), ACT.Exp).then_inc(s["qd_rdy"], 1)
                    act.wait_ge(s["arg_g"], t + 1)
                    for h in range(GH):
                        ins = act.activation(decT[:, h], decT[:, h], ACT.Exp, bias=ngc[:, t, h:h + 1])
                    ins.then_inc(s["dec_rdy"], 1)
                elif kind == "x":
                    act.wait_ge(s["x_ps"], n + 1)
                    act.copy(XW, bank[4][:].rearrange("p (h i) -> p h i", h=GH)).then_inc(s["x_out"], 1)
                elif kind == "nw":
                    act.wait_ge(s["nw_ps"], t + 1)
                    act.copy(XW, bank[4][:].rearrange("p (h i) -> p h i", h=GH)).then_inc(s["nw_out"], 1)
                elif kind == "vn":
                    act.wait_ge(s["vn_ps"], t + 1)
                    act.copy(kbT, bank[5][:].rearrange("p (h i) -> p h i", h=GH)).then_inc(s["vn_out"], 1)
                elif kind == "os":
                    act.wait_ge(s["os_ps"], t + 1)
                    act.copy(og[:, t], bank[6][:]).then_inc(s["os_out"], 1)

            for c in range(DC):
                act.wait_ge(s["mixT_ps"], c + 1)
                gain = sgc[:, 2:3] if c < 4 else ggc[:]
                act.activation(mixT[:, c], bank[c % 2][:], ACT.Copy, scale=gain).then_inc(s["mixT_out"], 1)
            for c in range(DC):
                act.wait_ge(s["h2T_ps"], c + 1)
                act.copy(h2T[:, c], bank[c % 2][:]).then_inc(s["h2T_out"], 1)
            for j in range(NS):
                act.wait_ge(s["q_ps"], j + 1)
                act.copy(qT[:, j], bank[j % 4][:]).then_inc(s["q_out"], 1)

            def queries(t):
                if not isinstance(t, int) or t > 0:
                    act.wait_ge(s["sc_ps"], t)
                act.copy(qs, qT[:, :, bass.ds(t * P, P)]).then_inc(s["qs_rdy"], 1)

            def softmax_exp(t, h):
                act.wait_ge(s["best_rdy"], t * PH + h + 1)
                act.activation(ebest, best, ACT.Exp, bias=nmax[:, 0:1], accum_out=esum[:, 0:1]).then_inc(s["e_out"], 1)

            act.wait_ge(s["q_ps"], NS)
            act.drain()
            queries(0)
            for h in range(PH - 2):
                softmax_exp(0, h)
            h2_flat = h2.rearrange("p t d -> p (t d)")

            def tile(i, has_next):
                act.wait_ge(s["u_free"], i * SEL + UB)
                for half in range(2):
                    ins = act.copy(bank[4 + half][:], h2_flat[:, bass.ds(i * D + half * 512, 512)])
                ins.then_inc(s["h2p_rdy"], 1)
                if has_next:
                    queries(i + 1)
                for h in range(PH + 1):
                    if h >= 1:
                        act.wait_ge(s["w_rdy"], i * PH + h)
                        for k in range(TOPK):
                            c = (h - 1) * TOPK + k
                            act.wait_ge(s["v_free"], SEL + i * SEL + c - VB + 1)
                            act.activation(diag[c % VB], ident[:], ACT.Copy, scale=wt[:, c:c + 1]).then_inc(s["diag_rdy"], 1)
                    if h == PH:
                        continue
                    c = slice(h * TOPK, (h + 1) * TOPK)
                    act.wait_ge(s["dots_rdy"], i * PH + h + 1)
                    act.activation(gel[:, c], dots[:, c], ACT.Gelu).then_inc(s["gel_rdy"], 1)
                    if h < 2:
                        softmax_exp(i, PH - 2 + h)
                    elif has_next:
                        softmax_exp(i + 1, h - 2)
                act.wait_ge(s["v_free"], SEL + i * SEL + SEL)
                act.wait_ge(s["stored"], 16 * (i + 1))
                for half in range(2):
                    ins = act.copy(y_s[:, half * 512:(half + 1) * 512], bank[6 + half][:])
                ins.then_inc(s["y_out"], 1)

            tiles(act, tile)

        @block.vector
        def _(dve):
            def rsqrt(dst, v, n, add):
                t = st[:, 2, 0:dst.shape[-1]]
                w = st[:, 1, 0:dst.shape[-1]]
                dve.tensor_scalar(w, v, n, add, ALU.mult, ALU.add)
                dve.drain()
                dve.tensor_scalar(dst.bitcast(I32), w.bitcast(I32), 1, None, ALU.arith_shift_right)
                dve.drain()
                dve.tensor_scalar(dst.bitcast(I32), dst.bitcast(I32), -1.0, float(0x5F3759DF), ALU.mult, ALU.add)
                dve.drain()
                for _ in range(3):
                    dve.tensor_tensor(t, dst, dst, ALU.mult)
                    dve.drain()
                    dve.scalar_tensor_tensor(t, t, -0.5, w, ALU.mult, ALU.mult)
                    dve.drain()
                    dve.scalar_tensor_tensor(dst, t, 1.5, dst, ALU.add, ALU.mult)
                    dve.drain()

            def norm_rows(v, heads, width, n, add, extra, tmp):
                k = NT * heads
                vv = v.rearrange("p t (h d) -> p (t h) d", h=heads)
                sv = tmp.rearrange("p (k d) -> p k d", k=k)
                dve.tensor_tensor(sv, vv, vv, ALU.mult)
                dve.drain()
                ss, rs = st[:, 3, 0:k], st[:, 0, 0:k]
                dve.tensor_reduce(ss, sv, AX.X, ALU.add)
                dve.drain()
                rsqrt(rs, ss, n, add)
                if extra != 1.0:
                    dve.tensor_scalar(rs, rs, extra, None, ALU.mult)
                    dve.drain()
                return dve.tensor_tensor(vv, vv, rs.unsqueeze(2).to_broadcast([P, k, width]), ALU.mult)

            dve.wait_ge(s["x_in"], 16)
            for t in range(NT):
                dve.tensor_tensor_reduce(xn[:, t], xs[:, t], xs[:, t], 1.0, 0.0, ALU.mult, ALU.add, st[:, 3, t:t + 1])
            dve.drain()
            rsqrt(st[:, 0, 0:NT], st[:, 3, 0:NT], 1.0 / D, EPS)
            for t in range(NT):
                dve.tensor_scalar(xn[:, t], xs[:, t], st[:, 0, t:t + 1], None, ALU.mult).then_inc(s["xn_rdy"], 1)
            dve.wait_ge(s["par_in"], 16 * NPAR)
            for dc in range(DC):
                dve.wait_ge(s["xT_ps"], dc + 1)
                dve.tensor_scalar(hT[:, dc], bank[4 + dc % 2][:], g1c[:, dc:dc + 1], None, ALU.mult).then_inc(s["hT_rdy"], 1)
            for r in raw:
                ins = dve.memset(r[:, 0:CONV - 1], 0.0)
            ins.then_inc(s["raw_clear"], 1)
            dve.wait_ge(s["ab_ps"], 1)
            dve.tensor_copy(ab[:], bank[7][:, 0:NT * 2 * GH].rearrange("p (t c) -> p t c", t=NT)).then_inc(s["ab_rdy"], 1)

            def conv_unit(i):
                dve.wait_ge(s["proj_out"], i + 1)
                if i >= 2:
                    dve.wait_ge(s["silu_done"], i - 1)
                r, c, w = raw[i % 2], conv[i % 2], cwc[:, i]
                dve.tensor_scalar(c, r[:, 0:T], w[:, 0:1], None, ALU.mult)
                for j in range(1, CONV):
                    dve.drain()
                    ins = dve.scalar_tensor_tensor(c, r[:, j:j + T], w[:, j:j + 1], c, ALU.mult, ALU.add)
                ins.then_inc(s["conv_done"], 1)

            for i in range(3 * GH):
                conv_unit(i)
                if i == 6:
                    dve.wait_ge(s["tr_out"], 4)
                    norm_rows(tok["gq"], GH, GD, 1.0, EPS, GD ** -0.5, squares).then_inc(s["gnorm"], 1)
                if i == 10:
                    dve.wait_ge(s["tr_out"], TR.index(("fwd", 7)) + 1)
                    dve.drain()
                    norm_rows(tok["gk"], GH, GD, 1.0, EPS, 1.0, squares).then_inc(s["gnorm"], 1)
            for j, name in enumerate(("sq", "sk")):
                dve.wait_ge(s["proj_out"], 4 * (BLOCKS.index(name) + 1))
                dve.drain()
                norm_rows(tok[name], SBH, SBD, 1.0 / SBD, EPS, SBD ** -0.5 if j == 0 else 1.0,
                          squares).then_inc(s["snorm"], 1)

            dve.tensor_tensor(gt1, ab[:, :, 0:GH], abc[:, GH:].unsqueeze(1).to_broadcast([P, NT, GH]), ALU.add)
            dve.drain()
            dve.scalar_tensor_tensor(gt2, gt1, -1.0, gt1, ALU.mult, ALU.min).then_inc(s["gate_dve"], 1)
            dve.wait_ge(s["gate_act"], 2)
            dve.scalar_tensor_tensor(gt1, gt1, 0.0, gt2, ALU.max, ALU.add)
            dve.tensor_scalar(gt3, gt3, 1.0, None, ALU.add)
            dve.tensor_scalar(st[:, 3, GH:2 * GH], st[:, 3, 0:GH], -1.0, None, ALU.mult)
            dve.drain()
            dve.reciprocal(beta, gt3)
            dve.tensor_tensor(g_, gt1, st[:, 3, GH:2 * GH].unsqueeze(1).to_broadcast([P, NT, GH]), ALU.mult).then_inc(s["gate_dve"], 1)
            dve.wait_ge(s["gate_act"], 3)
            dve.scalar_tensor_tensor(nbe, egc, -1.0, beta, ALU.mult, ALU.mult).then_inc(s["gate_dve"], 1)
            dve.memset(S, 0.0).then_inc(s["s_rdy"], 1)
            dve.drain()
            dve.engine_nop().then_inc(s["gate_dve"], 1)

            b4 = bank[4][:].rearrange("p (h i) -> p h i", h=GH)
            b5 = bank[5][:].rearrange("p (h i) -> p h i", h=GH)
            b6 = bank[6][:].rearrange("p (h i) -> p h i", h=GH)
            b7 = bank[7][:].rearrange("p (h i) -> p h i", h=GH)
            NL = len(LEVELS)

            def softplus_head(h):
                dve.wait_ge(s["l_rdy"], h + 1)
                if h >= 1:
                    dve.wait_ge(s["r_ps"], 3 * h)
                dve.scalar_tensor_tensor(sp_, zs[h % 2], 0.0, ez, ALU.max, ALU.add).then_inc(s["sp_rdy"], 1)

            for kind, t, i in B_ORDER:
                n = t * NL + i
                if kind == "z":
                    h, m = t, 3 * t + i
                    off, width, _ = PARTS[i]
                    dve.wait_ge(s["z_ps"], m + 1)
                    if i == 0 and h >= 2:
                        dve.wait_ge(s["wt_rdy"], h - 1)
                    dve.tensor_tensor(zs[h % 2][:, off:off + width], bank[m % 2][:, 0:width],
                                      sb_mask[:, off:off + width], ALU.add).then_inc(s["z_out"], 1)
                    if i == 2:
                        dve.drain()
                        dve.scalar_tensor_tensor(ez, zs[h % 2], -1.0, zs[h % 2], ALU.mult, ALU.min).then_inc(s["nabs_rdy"], 1)
                        if h == 0:
                            softplus_head(0)
                elif kind == "r":
                    h, m = t, 3 * t + i
                    off, width, _ = PARTS[i]
                    dve.wait_ge(s["r_ps"], m + 1)
                    z = zs[h % 2][:, off:off + width]
                    dve.tensor_tensor(z, z, bank[2][:, 0:width], ALU.subtract).then_inc(s["arg_rdy"], 1)
                    if i == 2 and h + 1 < SBH:
                        softplus_head(h + 1)
                elif kind == "bc":
                    dve.wait_ge(s["qd_rdy"], t + 1)
                    dve.drain()
                    dve.tensor_tensor(decT, b4, causal_add[:].unsqueeze(1).to_broadcast([P, GH, P]), ALU.add).then_inc(s["arg_g"], 1)
                    if t >= 1:
                        dve.wait_ge(s["os_ps"], t)
                    dve.tensor_tensor(kbT, gkT[:, :, t * P:(t + 1) * P], b5, ALU.mult).then_inc(s["kb_rdy"], 1)
                    dve.tensor_tensor(qdT, qdT, gqT[:, :, t * P:(t + 1) * P], ALU.mult)
                elif kind == "kk":
                    dve.wait_ge(s["kk_ps"], t + 1)
                    dve.wait_ge(s["dec_rdy"], t + 1)
                    if t >= 1:
                        dve.wait_ge(s["ats_rdy"], NL * t)
                    dve.tensor_tensor(AT, b6, decT, ALU.mult).then_inc(s["at_rdy"], 1)
                    dve.tensor_tensor(attnT, b7, decT, ALU.mult)
                elif kind == "y":
                    dve.wait_ge(s["y_ps"], n + 1)
                    dve.drain()
                    idb = ident[:].unsqueeze(1).to_broadcast([P, GH, P])
                    dve.tensor_tensor(TTI, TTI if i else idb, b6, ALU.subtract).then_inc(s["ti_rdy"], 1)
                    if i < NL - 1:
                        dve.tensor_tensor(TI, TI if i else idb, b5, ALU.subtract).then_inc(s["ti_rdy"], 1)
                    else:
                        dve.engine_nop().then_inc(s["ti_rdy"], 1)
                elif kind == "os":
                    dve.wait_ge(s["os_ps"], t + 1)
                    dve.drain()
                    dve.tensor_tensor(S, S, etot[:, t].unsqueeze(2).to_broadcast([P, GH, P]), ALU.mult)
                    dve.drain()
                    dve.tensor_tensor(S, S, b7, ALU.add).then_inc(s["s_rdy"], 1)

            dve.wait_ge(s["o_out"], SBH)
            dve.drain()
            sc = scratch.rearrange("p t d -> p (t d)")
            norm_rows(osb, SBH, SBD, 1.0 / SBD, EPS, 1.0, sc).then_inc(s["mix_rdy"], 1)
            dve.wait_ge(s["os_out"], NT)
            dve.drain()
            norm_rows(og, GH, GD, 1.0 / GD, EPS, 1.0, sc)
            dve.drain()
            dve.tensor_tensor(og, og, tok["z"], ALU.mult).then_inc(s["mix_rdy"], 1)
            for n in range(2 * NT):
                t, half = divmod(n, 2)
                dve.wait_ge(s["wo_ps"], n + 1)
                xv = xs[:, t, half * 512:(half + 1) * 512]
                dve.tensor_tensor(xv, xv, bank[4 + n % 4][:], ALU.add).then_inc(s["x2_rdy"], 1)
            dve.drain()
            for t in range(NT):
                dve.tensor_tensor_reduce(h2[:, t], xs[:, t], xs[:, t], 1.0, 0.0, ALU.mult, ALU.add, st[:, 3, t:t + 1])
            dve.drain()
            rsqrt(st[:, 0, 0:NT], st[:, 3, 0:NT], 1.0 / D, EPS)
            for t in range(NT):
                dve.scalar_tensor_tensor(h2[:, t], xs[:, t], st[:, 0, t:t + 1], g2b[:], ALU.mult, ALU.mult).then_inc(s["h2_rdy"], 1)

            dve.engine_nop().then_inc(s["u_free"], UB)
            dve.engine_nop().then_inc(s["v_free"], SEL)
            dve.engine_nop().then_inc(s["y_out"], 1)
            dve.engine_nop().then_inc(s["stored"], 16)
            idb16 = iota[:].unsqueeze(1).to_broadcast([P, TOPK, TOPK])

            def top16(out, idx, vals, left):
                for o, i_, v, l_ in zip(out, idx, vals, left):
                    dve.max(o[:, 0:8], v)
                dve.drain()
                for o, i_, v, l_ in zip(out, idx, vals, left):
                    dve.max_index(i_[:, 0:8], o[:, 0:8], v)
                    dve.match_replace(l_, o[:, 0:8], v, LOWEST)
                dve.drain()
                for o, i_, v, l_ in zip(out, idx, vals, left):
                    dve.max(o[:, 8:16], l_)
                dve.drain()
                for o, i_, v, l_ in zip(out, idx, vals, left):
                    ins = dve.max_index(i_[:, 8:16], o[:, 8:16], l_)
                return ins

            def choose(t, h):
                c = slice(h * TOPK, (h + 1) * TOPK)
                by_itself(dve, s["sc_ps"], t + 1)
                dve.drain()
                sc_ = [bank[(2 * h + a) // 4][:, ((2 * h + a) % 4) * NKEYS:((2 * h + a) % 4 + 1) * NKEYS] for a in range(2)]
                top16([top[:, 0], top[:, 1]], [topi[:, 0], topi[:, 1]], sc_, [rest[:, 0], rest[:, 1]])
                dve.tensor_tensor(cand.rearrange("p (a b) -> p a b", a=TOPK), top[:, 0].unsqueeze(2).to_broadcast([P, TOPK, TOPK]),
                                  top[:, 1].unsqueeze(1).to_broadcast([P, TOPK, TOPK]), ALU.add)
                dve.drain()
                top16([best], [pos], [cand], [crest])
                dve.tensor_scalar(nmax[:, 0:1], best[:, 0:1], -1.0, None, ALU.mult).then_inc(s["best_rdy"], 1)
                dve.drain()
                dve.tensor_scalar(pos1, pos, 4, None, ALU.logical_shift_right)
                dve.tensor_scalar(pos2, pos, TOPK - 1, None, ALU.bitwise_and)
                dve.drain()
                for e, q in ((eq1, pos1), (eq2, pos2)):
                    dve.tensor_tensor(e, q.unsqueeze(2).to_broadcast([P, TOPK, TOPK]), idb16, ALU.is_equal)
                dve.drain()
                for e, a in ((eq1, 0), (eq2, 1)):
                    dve.tensor_tensor(e, e, topi[:, a].unsqueeze(1).to_broadcast([P, TOPK, TOPK]), ALU.mult)
                dve.drain()
                dve.tensor_reduce(id1, eq1, AX.X, ALU.add)
                dve.tensor_reduce(id2, eq2, AX.X, ALU.add)
                dve.drain()
                by_itself(dve, s["v_free"], t * SEL + c.stop)
                dve.scalar_tensor_tensor(eid[:, c], id1, float(NKEYS), id2, ALU.mult, ALU.add).then_inc(s["eid_rdy"], 1)
                by_itself(dve, s["e_out"], t * PH + h + 1)
                dve.reciprocal(erec[:, 0:1], esum[:, 0:1])
                dve.drain()
                dve.tensor_scalar(gates[:, c], ebest, erec[:, 0:1], None, ALU.mult)

            for h in range(PH - 2):
                choose(0, h)

            def tile(i, has_next):
                for h in range(PH):
                    if h == 0:
                        dve.wait_ge(s["h2p_rdy"], i + 1)
                    for k in range(TOPK):
                        c = h * TOPK + k
                        by_itself(dve, u_in[c % UB], 16 * (i * (SEL // UB) + c // UB + 1))
                        dve.tensor_tensor_reduce(u_row[c % UB], u_row[c % UB], h2p, 1.0, 0.0, ALU.mult, ALU.add,
                                                 dots[:, c:c + 1]).then_inc(s["u_free"], 1)
                    dve.drain()
                    dve.engine_nop().then_inc(s["dots_rdy"], 1)
                    if h < 2:
                        choose(i, PH - 2 + h)
                    elif has_next:
                        choose(i + 1, h - 2)
                    c = slice(h * TOPK, (h + 1) * TOPK)
                    by_itself(dve, s["gel_rdy"], i * PH + h + 1)
                    dve.drain()
                    dve.tensor_tensor(wt[:, c], gel[:, c], gates[:, c], ALU.mult).then_inc(s["w_rdy"], 1)

            tiles(dve, tile)


NPAR = 5 + 6 + 1


_OUTS = ((1, T, D), "float32")


def kernel(**inputs):
    import numpy as _np
    import concourse.bacc as _bacc
    from concourse import mybir as _mybir
    from concourse.bass_utils import run_bass_kernel_spmd as _run

    a = {k: _np.asarray(v) for k, v in inputs.items()}
    a["norm1_g"] = a["norm1_g"][0].reshape(DC, P).T
    a["gdn_conv_w"] = a["gdn_conv_w"][0].reshape(CONV, 3 * GH, P).transpose(2, 1, 0)
    keys = _np.stack([a.pop("peer_keys1")[0], a.pop("peer_keys2")[0]], 1)
    a["keys_t"] = keys.reshape(1, NS, NKEYS, HALF).transpose(0, 1, 3, 2)

    nc = _bacc.Bacc("TRN2", target_bir_lowering=False, num_devices=1)
    arrays, args = {}, []
    for name in ("x", "norm1_g", "w_in", "sb_q_norm_g", "sb_k_norm_g", "sb_out_norm_g", "gdn_conv_w", "gdn_a_log",
                 "gdn_dt_bias", "gdn_out_norm_g", "w_out", "norm2_g", "peer_w_q", "keys_t", "peer_u", "peer_v"):
        v = _np.ascontiguousarray(a[name])
        arrays[f"in_{name}"] = v
        args.append(nc.dram_tensor(f"in_{name}", v.shape, _mybir.dt.from_np(v.dtype), kind="ExternalInput").ap())
    out = nc.dram_tensor("out_0", _OUTS[0], _mybir.dt.from_np(_np.dtype(_OUTS[1])), kind="ExternalOutput").ap()
    layer_kernel(nc, *args, out)
    r = _run(nc, [arrays], core_ids=[0])
    return r.results[0]["out_0"]
```

```python
import math
from contextlib import ExitStack

import concourse.bass as bass
from concourse import mybir

ALU = mybir.AluOpType
ACT = mybir.ActivationFunctionType
AX = mybir.AxisListType
F32 = mybir.dt.float32
I32 = mybir.dt.int32
U32 = mybir.dt.uint32

P = 128
D = 1024
T = 512
NT = T // P
DC = D // P
SBH, SBD = 8, 64
SBW = SBH * SBD
GH, GD = 4, 128
GW = GH * GD
CONV = 4
EPS = 1e-6
COL_GQ, COL_Z = 3 * SBW, 3 * SBW + 3 * GW
COL_AB = COL_Z + GW
PH, NKEYS, HALF, TOPK = 8, 128, 128, 16
NS = 2 * PH
SEL = PH * TOPK
NEG = -1.0e30
LOWEST = -3.0e38
LEVELS = [1 << i for i in range(7)]

KB_ORDER = [0, 1, 3, 2]
KB_OFF, _o = {}, 0
for _kb in KB_ORDER:
    KB_OFF[_kb] = _o
    _o += T - P * _kb
RAG = _o
PARTS = [(0, 512, [0]), (512, 512, [1, 3]), (1024, 256, [2])]

KB = 256

BLOCKS = ["gk", "gq", "gv", "z", "sq", "sk", "sv"]
BLOCK_COL = {"gq": COL_GQ, "gk": COL_GQ + GW, "gv": COL_GQ + 2 * GW, "z": COL_Z,
             "sq": 0, "sk": SBW, "sv": 2 * SBW}
NUNIT = 4 * len(BLOCKS)
NL = len(LEVELS)
NPAR = 4 + 6 + 1


def spread(main, extra):
    out, j = [], 0
    for i, m in enumerate(main):
        out.append(m)
        want = len(extra) * (i + 1) // len(main)
        out += extra[j:want]
        j = want
    return out


def stage_ab_order():
    proj = []
    for p in range(NUNIT):
        proj += [("proj", p, 0), ("proj", p, 1)]
        if 2 <= p < 14:
            proj.append(("fwd", p - 2, 0))
        if 8 <= p < 12:
            proj.append(("gback", p - 8, 0))
        if 14 <= p < 18:
            proj.append(("gback", p - 10, 0))
        if 21 <= p < 25:
            proj.append(("sback", p - 21, 0))
        if p >= 25:
            proj.append(("sback", p - 21, 0))
    proj.append(("sback", 7, 0))

    def inverse(t, rec):
        head = [("bc", t, 0), ("kk", t, 0)] + ([("qk", t, 0)] if t else [])
        levels = [(k, t, lv) for lv in range(NL) for k in ("x", "y")]
        return head + spread(levels, rec)

    def recur(t):
        return [("mul", t, 0), ("nw", t, 0), ("vn", t, 0), ("os", t, 0)]

    gdn = inverse(0, []) + [("qk", 0, 0)]
    for t in range(1, NT):
        gdn += inverse(t, recur(t - 1))
    gdn += recur(NT - 1)

    first = proj.index(("proj", 14, 0))
    late = proj[first:]
    halves = sum(k == "proj" for k, _, _ in late)
    out, j = proj[:first], 0
    for st_ in late:
        out.append(st_)
        if st_[0] == "proj":
            out.append(gdn[j])
            j += 1
    assert j == halves
    sb = []
    for h in range(SBH + 2):
        if h < SBH:
            sb += [("z", h, i) for i in range(3)]
        if 1 <= h <= SBH:
            sb += [("r", h - 1, i) for i in range(3)]
        if h >= 2:
            sb.append(("o", h - 2, 0))
    return out + spread(gdn[j:], sb)


def layer_kernel(nc, x, norm1_g, w_in, sb_q_norm_g, sb_k_norm_g, sb_out_norm_g, gdn_conv_w, gdn_a_log,
                 gdn_dt_bias, gdn_out_norm_g, w_out, norm2_g, peer_w_q, keys_t, peer_u, peer_v, out):
    x_d = x[0].rearrange("(t p) d -> p t d", p=P)
    out_d = out[0].rearrange("(t p) d -> p t d", p=P)
    w_in_d = w_in[0].rearrange("(c p) n -> p c n", p=P)
    w_out_d = w_out[0].rearrange("(c p) n -> p c n", p=P)
    w_q_d = peer_w_q[0].rearrange("(c p) n -> p c n", p=P)
    u_d, v_d = peer_u[0], peer_v[0]

    with ExitStack() as ctx:
        def sb(name, shape, dt=F32):
            return ctx.enter_context(nc.sbuf_tensor(name, shape, dt))

        def sem(name):
            return ctx.enter_context(nc.semaphore(name))

        arena = sb("arena", [P, 203 * KB])

        def at(kb, *shape):
            n = math.prod(shape)
            o = int(kb * KB)
            v = arena[:, o:o + n]
            if len(shape) == 2:
                v = v.rearrange("p (a b) -> p a b", a=shape[0])
            elif len(shape) == 3:
                v = v.rearrange("p (a b c) -> p a b c", a=shape[0], b=shape[1])
            return v

        xs = at(0, NT, D)
        hT = at(16, DC, T)
        wbuf = [at(32 + 16 * i, DC, 512) for i in range(2)]
        wab = at(80, DC, 2 * GH)
        tok = {"gq": at(80, NT, GW), "gk": at(88, NT, GW), "gv": at(96, NT, GW), "z": at(120, NT, GW),
               "sq": at(128, NT, SBW), "sk": at(136, NT, SBW), "sv": at(144, NT, SBW)}
        gqT, gkT = at(104, GH, T), at(112, GH, T)
        sqT, skT = at(152, SBH // 2, T), at(160, SBH // 2, T)
        xn = at(168, NT, D)
        raw = [at(168 + 2.25 * i, T + CONV - 1) for i in range(2)]
        conv = [at(173 + 2 * i, T) for i in range(2)]
        act_o = [at(177 + 2 * i, T) for i in range(2)]
        squares = at(182, NT * GW)
        sb_mask = at(190, RAG)
        lv_mask = at(195, NL, P)
        decT, kbT, AT, TI, ATs0, ATs1, XW, TT0 = (at(64 + 2 * i, GH, P) for i in range(8))
        ATs = [ATs0, ATs1]
        TT1, S, qd0, qd1, at0, at1 = (at(168 + 2 * i, GH, P) for i in range(6))
        TTI, qdT, attnT = [TT0, TT1], [qd0, qd1], [at0, at1]
        kd, nv = at(199, GW), at(201, GH, P)
        vb, kbe, og, osb = tok["gv"], tok["gk"], tok["gq"], tok["sq"]
        zs = [at(16 + 5 * i, RAG) for i in range(2)]
        ez, sp_ = at(26, RAG), at(31, RAG)
        wts = [at(36 + 5 * i, RAG) for i in range(2)]
        squares_b = at(62, GW)
        w_out_s = [at(k, D) for k in (46, 50, 54, 58, 136, 140, 182, 186)]
        mixT = at(16, NT, DC, P)
        squares_c = at(20, (NT - 1) * SBW)
        w_q_s = [at(k, NS * HALF) for k in (104, 112, 152, 160, 88, 96, 144, 120)]
        keysT = at(168, NS, NKEYS)
        UB, VB = 8, 8
        u_row = [at(k, D) for k in (36, 40, 64, 68, 72, 76, 80, 84)]
        v_row = [at(k, D) for k in (16, 20, 24, 28, 46, 50, 54, 58)]
        g2b = at(32, D)
        eid, eid_n = (at(44 + 0.5 * i, SEL).bitcast(U32) for i in range(2))
        gates, gates_n = (at(45 + 0.5 * i, SEL) for i in range(2))
        dots, gel, wt = (at(180 + 0.5 * i, SEL) for i in range(3))
        y_s = at(136, D)
        diag = [at(140 + 0.5 * i, P) for i in range(VB)]
        qs = at(190, NS, P)
        h2sq = at(190, D)
        h2 = at(176, D)
        h2T = at(199, DC, P)
        top = at(128, 2, TOPK)
        topi = at(128.25, 2, TOPK).bitcast(U32)
        rest = at(129, 2, NKEYS)
        cand, crest = at(130, TOPK * TOPK), at(131, TOPK * TOPK)
        eq1, eq2 = at(132, TOPK, TOPK), at(133, TOPK, TOPK)
        best, id1, id2, esum, erec = (at(134 + i * 0.0625, TOPK) for i in range(5))
        pos, pos1, pos2 = (at(135 + i * 0.0625, TOPK).bitcast(U32) for i in range(3))

        iota = sb("iota", [P, TOPK])
        ident = sb("ident", [P, P])
        ones = sb("ones", [P, P])
        tri_ge = sb("tri_ge", [P, P])
        tri_gt = sb("tri_gt", [P, P])
        tri_le = sb("tri_le", [P, P])
        causal_add = sb("causal_add", [P, P])
        g1c = sb("g1c", [P, DC])
        sgc = sb("sgc", [P, 3])
        ggc = sb("ggc", [P, 1])
        cwc = sb("cwc", [P, 3 * GH, CONV])
        abc = sb("abc", [P, 2 * GH])
        st = sb("st", [P, 4, 32])
        ab = sb("ab", [P, NT, 2 * GH])
        gt = sb("gt", [P, 10, NT, GH])
        g_, beta, ngc, egc, nbe, ekd, etot, gt1, gt2, gt3 = (gt[:, i] for i in range(10))

        psum = ctx.enter_context(nc.psum_tensor("psum", [P, 8, 512], F32))
        bank = [psum[:, i] for i in range(8)]

        u_in = [sem(f"u_in{i}") for i in range(UB)]
        v_in = [sem(f"v_in{i}") for i in range(VB)]
        s = {n: sem(n) for n in (
            "y_out", "stored", "dve_turns", "pool_turns", "sc_ps", "picked", "best_rdy", "e_out", "eid_rdy", "u_free", "v_free",
            "h2p_rdy", "gel_rdy", "dots_rdy", "w_rdy", "diag_rdy",
            "x_in", "par_in", "w0_in", "w1_in", "wab_in", "wout_in", "wq_in", "keys_in", "g2_in",
            "consts", "xn_rdy", "xT_ps", "hT_rdy", "ab_ps", "ab_rdy",
            "proj_ps", "proj_out", "conv_done", "silu_done", "tr_ps", "tr_out", "gnorm", "snorm",
            "raw_clear", "raw_free", "gate_dve", "gate_act", "gate_ps", "mul_rdy", "qk_ps", "attn_rdy",
            "z_ps", "z_out", "nabs_rdy", "e_rdy", "l_rdy", "sp_rdy", "r_ps", "arg_rdy", "wt_rdy",
            "o_ps", "o_out",
            "bc_ps", "arg_g", "dec_rdy", "kb_rdy", "qd_rdy", "kk_ps", "at_rdy", "ats_rdy",
            "x_ps", "x_out", "y_ps", "ti_rdy", "nw_ps", "nw_out", "vn_ps", "vn_out", "os_ps", "os_out",
            "s_rdy", "mix_rdy", "mixT_ps", "mixT_out", "wo_ps", "x2_rdy", "h2_rdy", "h2T_ps", "h2T_out",
            "q_ps", "q_out")}
        ORDER = stage_ab_order()
        TR = [step for step in ORDER if step[0] in ("fwd", "gback", "sback")]

        def count(kind, until):
            return sum(step[0] == kind for step in ORDER[:until])

        def heads(v):
            return v.rearrange("p (h i) -> p h i", h=GH)

        h2p = psum[:, 4:6].rearrange("p a b -> p (a b)")

        def by_itself(eng, semaphore, value):
            eng.wait_ge(semaphore, value)
            eng.sem_inc(s["dve_turns" if eng is nc.vector else "pool_turns"], 1)

        def tiles(eng, body):
            body(0)
            with eng.Fori(1, NT - 1) as i:
                body(i)
            body(NT - 1)

        EARLY = 1
        FIRST_AT = [5, 18, 22, 26, 34, 40, 46]
        GROUPS0 = [(0, 1, None, None), (1, 5, 12, 1), (5, 8, 36, 3)]
        TURN_AT, QUERY_AT = 2 * TOPK, 2 * TOPK + 4
        SCORE_AT = QUERY_AT + 2 * NS
        NEXT_AT = SCORE_AT + TOPK + 4
        EXP_AT = NEXT_AT + 5 * PH - 1 - TOPK

        def chosen_after(i, c):
            if is_first(i) and c in FIRST_AT:
                return 0, EARLY + FIRST_AT.index(c)
            n, left = divmod(c - NEXT_AT, 5)
            if not is_last(i) and n in range(PH) and left == 0:
                return 1, n
            return None

        def wo_bank(n):
            return 4 + n if n < 4 else 6 + n % 2

        def is_first(i):
            return isinstance(i, int) and i == 0

        def is_last(i):
            return isinstance(i, int) and i == NT - 1

        block = ctx.enter_context(nc.Block())

        @block.sync
        def _(sp):
            sp.dma_start(xs, x_d).then_inc(s["x_in"], 16)
            sp.dma_start(wab, w_in_d[:, :, COL_AB:COL_AB + 2 * GH]).then_inc(s["wab_in"], 16)
            pars = [(g1c[:], norm1_g),
                    (ggc[:], gdn_out_norm_g[0].rearrange("(p o) -> p o", o=1)),
                    (abc[:, 0:GH], gdn_a_log[0].partition_broadcast(P)),
                    (abc[:, GH:2 * GH], gdn_dt_bias[0].partition_broadcast(P))]
            for i, g in enumerate((sb_q_norm_g, sb_k_norm_g, sb_out_norm_g)):
                for half in range(2):
                    pars.append((sgc[half * SBD:(half + 1) * SBD, i:i + 1],
                                 g[0].rearrange("(p o) -> p o", o=1)))
            pars.append((cwc[:], gdn_conv_w))
            assert len(pars) == NPAR
            for dst, src in pars:
                sp.dma_start(dst, src).then_inc(s["par_in"], 16)
            for b, name in enumerate(BLOCKS):
                if b >= 2:
                    sp.wait_ge(s["proj_ps"], 4 * (b - 1))
                c0 = BLOCK_COL[name]
                sp.dma_start(wbuf[b % 2], w_in_d[:, :, c0:c0 + 512]).then_inc(s[f"w{b % 2}_in"], 16)
            sp.wait_ge(s["proj_ps"], NUNIT)
            sp.wait_ge(s["tr_ps"], len(TR))
            sp.wait_ge(s["snorm"], 2 * NT)
            for c in range(DC):
                sp.dma_start(w_out_s[c], w_out_d[:, c]).then_inc(s["wout_in"], 16)
            for c in range(DC):
                if c == 0:
                    sp.wait_ge(s["attn_rdy"], NT)
                elif c == 2:
                    sp.wait_ge(s["z_ps"], 3 * SBH)
                elif c == 4:
                    sp.wait_ge(s["vn_ps"], NT)
                elif c == 6:
                    sp.wait_ge(s["o_ps"], SBH)
                    sp.wait_ge(s["s_rdy"], NT + 1)
                    sp.dma_start(g2b, norm2_g[0].partition_broadcast(P)).then_inc(s["g2_in"], 16)
                    sp.dma_start(keysT, keys_t[0].rearrange("a d n -> d a n")).then_inc(s["keys_in"], 16)
                elif c == 7:
                    sp.wait_ge(s["mix_rdy"], 2)
                sp.dma_start(w_q_s[c], w_q_d[:, c]).then_inc(s["wq_in"], 16)
            with sp.Fori(0, NT) as i:
                sp.wait_ge(s["y_out"], i + 2)
                sp.dma_start(out_d[:, bass.ds(i, 1)].rearrange("p o d -> p (o d)"), y_s).then_inc(s["stored"], 16)
            sp.wait_ge(s["stored"], 16 * (NT + 1))

        @block.gpsimd
        def _(pool):
            pool.memset(ones[:], 1.0)
            pool.memset(sb_mask, 0.0)
            pool.memset(causal_add[:], 0.0)
            pool.memset(lv_mask, 1.0)
            pool.drain()

            def tri(dst, src, op, base, cm, step, fill):
                return pool.affine_select(out=dst, in_=src, compare_op=op, fill=fill, base=base,
                                          pattern=[[step, P]], channel_multiplier=cm)
            tri(ident[:], ones[:], ALU.is_equal, 0, 1, -1, 0.0)
            tri(tri_ge[:], ones[:], ALU.is_ge, 0, 1, -1, 0.0)
            tri(tri_gt[:], ones[:], ALU.is_gt, 0, 1, -1, 0.0)
            tri(tri_le[:], ones[:], ALU.is_ge, 0, -1, 1, 0.0)
            tri(causal_add[:], causal_add[:], ALU.is_ge, 0, -1, 1, NEG)
            for kb in range(NT):
                o = sb_mask[:, KB_OFF[kb]:KB_OFF[kb] + P]
                tri(o, o, ALU.is_gt, 0, -1, 1, NEG)
            for lv, z in enumerate(LEVELS):
                n = P // (2 * z)
                m = lv_mask[:, lv].rearrange("p (b h z) -> p b h z", b=n, h=2)
                pool.memset(m[:, :, 0], 0.0)
                pool.drain()
                pool.affine_select(out=m, in_=m, compare_op=ALU.is_ge, fill=0.0, base=0,
                                   pattern=[[-2 * z, n], [0, 2], [0, z]], channel_multiplier=1)
                pool.drain()
                last = pool.affine_select(out=m, in_=m, compare_op=ALU.is_ge, fill=0.0, base=z - 1,
                                          pattern=[[2 * z, n], [0, 2], [0, z]], channel_multiplier=-1)
            pool.iota(iota[:], pattern=[[1, TOPK]], base=0, channel_multiplier=0,
                      allow_small_or_imprecise_dtypes=True)
            pool.drain()
            pool.engine_nop().then_inc(s["consts"], 1)

            def level_mask(t, lv):
                n = t * NL + lv
                if lv == 0:
                    pool.wait_ge(s["at_rdy"], t + 1)
                if n >= 2:
                    pool.wait_ge(s["x_ps"], n - 1)
                pool.tensor_tensor(ATs[n % 2], AT, lv_mask[:, lv].unsqueeze(1).to_broadcast([P, GH, P]),
                                   ALU.mult).then_inc(s["ats_rdy"], 1)

            def on_rows(dst, src, gate, t):
                return pool.tensor_tensor(heads(dst), heads(src), gate[:, t].unsqueeze(2).to_broadcast([P, GH, GD]),
                                          ALU.mult)

            for kind, t, i in ORDER:
                if kind == "kk":
                    level_mask(t, 0)
                    level_mask(t, 1)
                elif kind == "x" and i + 2 < NL:
                    level_mask(t, i + 2)
                elif kind == "mul":
                    if t == 0:
                        pool.wait_ge(s["gate_dve"], 4)
                        pool.wait_ge(s["tr_out"], max(TR.index(("gback", 3, 0)), TR.index(("fwd", 11, 0))) + 1)
                        pool.wait_ge(s["raw_free"], 1)
                    else:
                        pool.wait_ge(s["os_ps"], t)
                    on_rows(kd, tok["gk"][:, t], ekd, t)
                    on_rows(vb[:, t], vb[:, t], beta, t)
                    pool.drain()
                    on_rows(kbe[:, t], kbe[:, t], nbe, t).then_inc(s["mul_rdy"], 1)

            def gather(buf, table, col, landed):
                pool.indirect_dma_start(buf, None, table, bass.IndirectOffsetOnAxis(ap=eid[:, col:col + 1], axis=0)
                                        ).then_inc(landed, 16)

            def gather_v(row, c):
                by_itself(pool, s["v_free"], SEL + row + c - VB + 1)
                gather(v_row[c % VB], v_d, c, v_in[c % VB])

            def tile(i):
                for h in range(PH):
                    by_itself(pool, s["eid_rdy"], i * PH + h + 1)
                    if is_first(i) and h == 1:
                        pool.wait_ge(s["wo_ps"], 2 * NT)
                    for k in range(TOPK):
                        c = h * TOPK + k
                        by_itself(pool, s["u_free"], i * SEL + c + 1)
                        gather(u_row[c % UB], u_d, c, u_in[c % UB])
                        if h >= 1:
                            gather_v(i * SEL, (h - 1) * TOPK + k)
                        elif not is_first(i):
                            gather_v((i - 1) * SEL, (PH - 1) * TOPK + k)

            pool.wait_ge(s["mixT_ps"], NT)
            tiles(pool, tile)
            for k in range(TOPK):
                gather_v((NT - 1) * SEL, (PH - 1) * TOPK + k)

        @block.tensor
        def _(pe):
            pe.wait_ge(s["consts"], 1)
            for dc in range(DC):
                if dc == 0:
                    pe.wait_ge(s["xn_rdy"], NT)
                if dc >= 2:
                    pe.wait_ge(s["hT_rdy"], dc - 1)
                for t in range(NT):
                    mm = pe.transpose(bank[4 + dc % 2][:, t * P:(t + 1) * P], xn[:, t, dc * P:(dc + 1) * P], ident[:])
                mm.then_inc(s["xT_ps"], 1)
            pe.wait_ge(s["hT_rdy"], DC)
            pe.wait_ge(s["wab_in"], 16)
            for t in range(NT):
                for dc in range(DC):
                    mm = pe.matmul(bank[7][:, t * 2 * GH:(t + 1) * 2 * GH], hT[:, dc, t * P:(t + 1) * P],
                                   wab[:, dc], start=dc == 0, stop=dc == DC - 1)
            mm.then_inc(s["ab_ps"], 1)
            pe.wait_ge(s["gate_dve"], 2)
            gall = g_.rearrange("p t h -> p (t h)")
            pe.matmul(bank[3][:, 0:16], tri_le[:], gall, start=True, stop=True)
            pe.matmul(bank[3][:, 16:32], tri_gt[:], gall, start=True, stop=True)
            pe.matmul(bank[3][:, 32:48], ones[:], gall, start=True, stop=True).then_inc(s["gate_ps"], 1)

            def project(p, half):
                b, u = divmod(p, 4)
                if half == 0:
                    if u == 0:
                        pe.wait_ge(s[f"w{b % 2}_in"], 16 * (b // 2 + 1))
                    if p >= 2:
                        pe.wait_ge(s["proj_out"], p - 1)
                w, ps = wbuf[b % 2], bank[p % 2]
                for dc in range(half * DC // 2, (half + 1) * DC // 2):
                    if b < 3:
                        mm = pe.matmul(ps, w[:, dc, u * P:(u + 1) * P], hT[:, dc], start=dc == 0, stop=dc == DC - 1)
                    else:
                        mm = pe.matmul(ps, hT[:, dc, u * P:(u + 1) * P], w[:, dc], start=dc == 0, stop=dc == DC - 1)
                if half == 1:
                    mm.then_inc(s["proj_ps"], 1)

            def turn(kind, i):
                n = TR.index((kind, i, 0))
                if n >= 1:
                    pe.wait_ge(s["tr_out"], n)
                if kind == "fwd":
                    pe.wait_ge(s["silu_done"], i + 1)
                elif kind == "gback":
                    pe.wait_ge(s["gnorm"], i // GH + 1)
                else:
                    pe.wait_ge(s["snorm"], NT * (i // 4 + 1))
                for t in range(NT):
                    if kind == "fwd":
                        src = act_o[i % 2][:, t * P:(t + 1) * P]
                    elif kind == "gback":
                        src = tok["gk" if i < GH else "gq"][:, t, (i % GH) * GD:(i % GH + 1) * GD]
                    else:
                        src = tok["sq" if i < 4 else "sk"][:, t, (i % 4) * P:(i % 4 + 1) * P]
                    mm = pe.transpose(bank[2][:, t * P:(t + 1) * P], src, ident[:])
                mm.then_inc(s["tr_ps"], 1)

            def attention(kind, h, i):
                off, width, kbs = PARTS[i]
                n = 3 * h + i
                if kind == "z":
                    if n == 0:
                        pe.wait_ge(s["tr_out"], len(TR))
                        pe.wait_ge(s["proj_out"], NUNIT)
                    else:
                        pe.wait_ge(s["z_out"], n)
                    r = slice((h % 2) * SBD, (h % 2 + 1) * SBD)
                    for kb in kbs:
                        o = KB_OFF[kb] - off
                        mm = pe.matmul(bank[0][:, o:o + T - kb * P], skT[r, h // 2, kb * P:(kb + 1) * P],
                                       sqT[r, h // 2, kb * P:T], start=True, stop=True)
                    mm.then_inc(s["z_ps"], 1)
                elif kind == "r":
                    if i == 0:
                        pe.wait_ge(s["sp_rdy"], h + 1)
                    if n >= 1:
                        pe.wait_ge(s["arg_rdy"], n)
                    ops = []
                    for kb in kbs:
                        o = KB_OFF[kb] - off
                        ops.append((tri_ge, o, KB_OFF[kb], T - kb * P))
                        for k2 in range(kb + 1, NT):
                            ops.append((ones, o + (k2 - kb) * P, KB_OFF[k2], T - k2 * P))
                    for j, (m, o, src, w) in enumerate(ops):
                        mm = pe.matmul(bank[1][:, o:o + w], m[:], sp_[:, src:src + w], start=j == 0,
                                       stop=j == len(ops) - 1, skip_group_check=True)
                    mm.then_inc(s["r_ps"], 1)
                else:
                    pe.wait_ge(s["wt_rdy"], h + 1)
                    if h >= 1:
                        pe.wait_ge(s["o_out"], h)
                    for qt in range(NT):
                        for kb in range(qt + 1):
                            o = KB_OFF[kb] + (qt - kb) * P
                            mm = pe.matmul(bank[2][:, qt * SBD:(qt + 1) * SBD], wts[h % 2][:, o:o + P],
                                           tok["sv"][:, kb, h * SBD:(h + 1) * SBD], start=kb == 0, stop=kb == qt)
                    mm.then_inc(s["o_ps"], 1)

            for at_step, (kind, t, i) in enumerate(ORDER):
                n = t * NL + i
                if kind == "proj":
                    project(t, i)
                elif kind in ("fwd", "gback", "sback"):
                    turn(kind, t)
                elif kind in ("z", "r", "o"):
                    attention(kind, t, i)
                elif kind == "bc":
                    if t == 0:
                        pe.wait_ge(s["gate_dve"], 4)
                    else:
                        pe.wait_ge(s["ti_rdy"], 2 * NL * t)
                    for h in range(GH):
                        c = slice(h * P, (h + 1) * P)
                        pe.matmul(bank[4][:, c], g_[:, t, h:h + 1].to_broadcast([P, P]), tri_le[:], start=True, stop=True)
                        mm = pe.matmul(bank[5][:, c], beta[:, t, h:h + 1].to_broadcast([P, P]), ident[:],
                                       start=True, stop=True)
                    mm.then_inc(s["bc_ps"], 1)
                elif kind == "kk":
                    pe.wait_ge(s["kb_rdy"], t + 1)
                    for h in range(GH):
                        mm = pe.matmul(bank[6][:, h * P:(h + 1) * P], gkT[:, h, t * P:(t + 1) * P], kbT[:, h],
                                       start=True, stop=True)
                    mm.then_inc(s["kk_ps"], 1)
                elif kind == "qk":
                    if t == 0:
                        pe.wait_ge(s["tr_out"], TR.index(("gback", 7, 0)) + 1)
                    if count("os", at_step):
                        pe.wait_ge(s["s_rdy"], count("os", at_step) + 1)
                    if count("nw", at_step):
                        pe.wait_ge(s["nw_out"], count("nw", at_step))
                    for h in range(GH):
                        mm = pe.matmul(bank[7][:, h * P:(h + 1) * P], gkT[:, h, t * P:(t + 1) * P],
                                       gqT[:, h, t * P:(t + 1) * P], start=True, stop=True)
                    mm.then_inc(s["qk_ps"], 1)
                elif kind == "x":
                    pe.wait_ge(s["ats_rdy"], n + 1)
                    if i >= 1:
                        pe.wait_ge(s["ti_rdy"], 2 * n)
                    for h in range(GH):
                        mm = pe.matmul(bank[4][:, h * P:(h + 1) * P], ATs[n % 2][:, h], TI[:, h] if i else ident[:],
                                       start=True, stop=True)
                    mm.then_inc(s["x_ps"], 1)
                elif kind == "y":
                    pe.wait_ge(s["x_out"], n + 1)
                    for h in range(GH):
                        c = slice(h * P, (h + 1) * P)
                        tt = TTI[t % 2][:, h] if i else ident[:]
                        if i < NL - 1:
                            pe.matmul(bank[5][:, c], tt, XW[:, h], start=True, stop=True)
                        mm = pe.matmul(bank[6][:, c], XW[:, h], tt, start=True, stop=True)
                    mm.then_inc(s["y_ps"], 1)
                elif kind == "nw":
                    pe.wait_ge(s["ti_rdy"], 2 * NL * (t + 1))
                    pe.wait_ge(s["mul_rdy"], t + 1)
                    pe.wait_ge(s["attn_rdy"], count("qk", at_step))
                    pe.wait_ge(s["s_rdy"], t + 1)
                    for h in range(GH):
                        mm = pe.matmul(bank[7][:, h * P:(h + 1) * P], kbe[:, t, h * GD:(h + 1) * GD], TTI[t % 2][:, h],
                                       start=True, stop=True)
                    mm.then_inc(s["nw_ps"], 1)
                elif kind == "vn":
                    pe.wait_ge(s["nw_out"], t + 1)
                    if t >= 1:
                        pe.wait_ge(s["os_out"], t)
                    for h in range(GH):
                        c = slice(h * P, (h + 1) * P)
                        pe.matmul(bank[3][:, c], TTI[t % 2][:, h], vb[:, t, h * GD:(h + 1) * GD], start=True, stop=False)
                        mm = pe.matmul(bank[3][:, c], nv[:, h], S[:, h], start=False, stop=True)
                    mm.then_inc(s["vn_ps"], 1)
                elif kind == "os":
                    pe.wait_ge(s["vn_out"], t + 1)
                    pe.wait_ge(s["attn_rdy"], count("qk", at_step))
                    for h in range(GH):
                        c = slice(h * P, (h + 1) * P)
                        pe.matmul(bank[3][:, c], qdT[t % 2][:, h], S[:, h], start=True, stop=False)
                        pe.matmul(bank[3][:, c], attnT[t % 2][:, h], nv[:, h], start=False, stop=True)
                        mm = pe.matmul(bank[7][:, c], kd[:, h * GD:(h + 1) * GD], nv[:, h], start=True, stop=True)
                    mm.then_inc(s["os_ps"], 1)

            def turn_mix(t):
                if t <= 1:
                    pe.wait_ge(s["mix_rdy"], 3 if t else 1)
                else:
                    pe.wait_ge(s["mixT_out"], t - 1)
                for c in range(DC):
                    src = osb[:, t, c * P:(c + 1) * P] if c < 4 else og[:, t, (c - 4) * P:(c - 3) * P]
                    mm = pe.transpose(bank[2 * (t % 2) + c // 4][:, (c % 4) * P:(c % 4 + 1) * P], src, ident[:])
                mm.then_inc(s["mixT_ps"], 1)

            def mix_out(n):
                t, half = divmod(n, 2)
                pe.wait_ge(s["mixT_out"], t + 1)
                if n >= 4:
                    pe.wait_ge(s["x2_rdy"], n - 1)
                for c in range(DC):
                    mm = pe.matmul(bank[wo_bank(n)], mixT[:, t, c], w_out_s[c][:, half * 512:(half + 1) * 512],
                                   start=c == 0, stop=c == DC - 1)
                mm.then_inc(s["wo_ps"], 1)

            turn_mix(0)
            pe.wait_ge(s["wout_in"], 16 * DC)
            mix_out(0)
            mix_out(1)
            for t in range(1, NT):
                turn_mix(t)
            mix_out(2)
            pe.wait_ge(s["mixT_out"], NT)
            def turn_h2(t):
                pe.wait_ge(s["h2_rdy"], t + 1)
                for c in range(DC):
                    mm = pe.transpose(bank[c // 4][:, (c % 4) * P:(c % 4 + 1) * P], h2[:, c * P:(c + 1) * P], ident[:])
                mm.then_inc(s["h2T_ps"], 1)

            def query(j, part, parts):
                for c in range(part * DC // parts, (part + 1) * DC // parts):
                    mm = pe.matmul(bank[j // 4][:, (j % 4) * P:(j % 4 + 1) * P], w_q_s[c][:, j * HALF:(j + 1) * HALF],
                                   h2T[:, c], start=c == 0, stop=c == DC - 1)
                return mm

            def scores(t):
                pe.wait_ge(s["q_out"], t + 1)
                for j in range(NS):
                    mm = pe.matmul(bank[j // 4][:, (j % 4) * NKEYS:(j % 4 + 1) * NKEYS], qs[:, j], keysT[:, j],
                                   start=True, stop=True)
                mm.then_inc(s["sc_ps"], 1)

            turn_h2(0)
            pe.wait_ge(s["wq_in"], 16 * DC)
            pe.wait_ge(s["h2T_out"], 1)
            for j in range(NS):
                mm = query(j, 0, 1)
            mm.then_inc(s["q_ps"], 1)
            pe.wait_ge(s["keys_in"], 16)
            scores(0)
            for n in range(3, 2 * NT):
                mix_out(n)
            x2 = xs.rearrange("p t d -> p (t d)")

            def tile(i):
                pe.wait_ge(s["y_out"], i + 1)
                if is_first(i):
                    pe.wait_ge(s["x2_rdy"], 2 * NT)
                for half in range(2):
                    pe.matmul(bank[6 + half], ident[:], x2[:, bass.ds(i * D + half * 512, 512)], start=True,
                              stop=False, skip_group_check=True)
                for c in range(SEL):
                    if not is_last(i):
                        if c == TURN_AT:
                            pe.wait_ge(s["picked"], (i + 1) * PH)
                            turn_h2(i + 1)
                        if QUERY_AT <= c < SCORE_AT:
                            if c == QUERY_AT:
                                pe.wait_ge(s["h2T_out"], i + 2)
                            mm = query((c - QUERY_AT) // 2, (c - QUERY_AT) % 2, 2)
                            if c == SCORE_AT - 1:
                                mm.then_inc(s["q_ps"], 1)
                        if c == SCORE_AT:
                            scores(i + 1)
                    pe.wait_ge(s["diag_rdy"], i * SEL + c + 1)
                    pe.wait_ge(v_in[c % VB], 16 * (i * (SEL // VB) + c // VB + 1))
                    for half in range(2):
                        mm = pe.matmul(bank[6 + half], diag[c % VB], v_row[c % VB][:, half * 512:(half + 1) * 512],
                                       start=False, stop=c == SEL - 1, skip_group_check=True)
                    mm.then_inc(s["v_free"], 1)

            tiles(pe, tile)

        @block.scalar
        def _(act):
            act.preload_act_table_set("natural_log_exp_and_others")
            act.wait_ge(s["par_in"], 16 * NPAR)
            act.activation(st[:, 3, 4 * GH:5 * GH], abc[:, 0:GH], ACT.Exp).then_inc(s["gate_act"], 1)
            act.wait_ge(s["gate_dve"], 1)
            act.activation(gt2, gt2, ACT.Exp)
            act.activation(gt3, ab[:, :, GH:], ACT.Exp, scale=-1.0)
            act.drain()
            act.activation(gt2, gt2, ACT.Ln, bias=1.0).then_inc(s["gate_act"], 1)
            act.wait_ge(s["gate_ps"], 1)
            sums = bank[3][:, 0:48].rearrange("p (a t h) -> p a t h", a=3, t=NT)
            act.mul(ngc, sums[:, 0], -1.0)
            act.activation(egc, sums[:, 0], ACT.Exp)
            act.activation(ekd, sums[:, 1], ACT.Exp)
            act.activation(etot, sums[:, 2], ACT.Exp).then_inc(s["gate_act"], 1)

            def projected(p):
                b, u = divmod(p, 4)
                act.wait_ge(s["proj_ps"], p + 1)
                if b < 3:
                    act.wait_ge(s["raw_clear"], 1)
                    if p >= 2:
                        act.wait_ge(s["conv_done"], p - 1)
                    act.copy(raw[p % 2][:, CONV - 1:], bank[p % 2]).then_inc(s["proj_out"], 1)
                elif BLOCKS[b] == "z":
                    act.activation(tok["z"][:, u], bank[p % 2], ACT.Silu).then_inc(s["proj_out"], 1)
                    if u == 3:
                        act.preload_act_table_set("natural_log_exp_and_others")
                else:
                    act.copy(tok[BLOCKS[b]][:, u], bank[p % 2]).then_inc(s["proj_out"], 1)
                if 1 <= p <= 12:
                    j = p - 1
                    act.wait_ge(s["conv_done"], j + 1)
                    if j >= 2:
                        act.wait_ge(s["tr_ps"], TR.index(("fwd", j - 2, 0)) + 1)
                    act.activation(act_o[j % 2], conv[j % 2], ACT.Silu).then_inc(s["silu_done"], 1)

            def turned(kind, i):
                n = TR.index((kind, i, 0))
                act.wait_ge(s["tr_ps"], n + 1)
                if kind == "fwd":
                    h = i % GH
                    dst = tok[BLOCKS[i // GH]][:, :, h * GD:(h + 1) * GD]
                    ins = act.copy(dst, bank[2].rearrange("p (t d) -> p t d", t=NT))
                elif kind == "gback":
                    ins = act.copy((gkT if i < GH else gqT)[:, i % GH], bank[2])
                else:
                    ins = act.activation((sqT if i < 4 else skT)[:, i % 4], bank[2], ACT.Copy,
                                         scale=sgc[:, i // 4:i // 4 + 1])
                ins.then_inc(s["tr_out"], 1)

            for kind, t, i in ORDER:
                n = t * NL + i
                if kind == "proj":
                    if i == 1:
                        projected(t)
                elif kind in ("fwd", "gback", "sback"):
                    turned(kind, t)
                elif kind == "z" and i == 2:
                    h = t
                    act.wait_ge(s["nabs_rdy"], h + 1)
                    act.activation(ez, ez, ACT.Exp).then_inc(s["e_rdy"], 1)
                    act.wait_ge(s["e_rdy"], h + 1)
                    act.activation(ez, ez, ACT.Ln, bias=1.0).then_inc(s["l_rdy"], 1)
                elif kind == "r" and i == 2:
                    h = t
                    act.wait_ge(s["arg_rdy"], 3 * h + 3)
                    if h >= 2:
                        act.wait_ge(s["o_ps"], h - 1)
                    act.activation(wts[h % 2], zs[h % 2], ACT.Exp).then_inc(s["wt_rdy"], 1)
                elif kind == "o":
                    h = t
                    act.wait_ge(s["o_ps"], h + 1)
                    act.copy(osb[:, :, h * SBD:(h + 1) * SBD],
                             bank[2][:, 0:NT * SBD].rearrange("p (t d) -> p t d", t=NT)).then_inc(s["o_out"], 1)
                elif kind == "bc":
                    act.wait_ge(s["bc_ps"], t + 1)
                    if t == 0:
                        act.wait_ge(s["raw_free"], 1)
                    if t >= 2:
                        act.wait_ge(s["os_ps"], t - 1)
                    act.activation(qdT[t % 2], heads(bank[4]), ACT.Exp).then_inc(s["qd_rdy"], 1)
                    act.wait_ge(s["arg_g"], t + 1)
                    for h in range(GH):
                        ins = act.activation(decT[:, h], decT[:, h], ACT.Exp, bias=ngc[:, t, h:h + 1])
                    ins.then_inc(s["dec_rdy"], 1)
                elif kind == "x":
                    act.wait_ge(s["x_ps"], n + 1)
                    act.copy(XW, heads(bank[4])).then_inc(s["x_out"], 1)
                elif kind == "nw":
                    act.wait_ge(s["nw_ps"], t + 1)
                    if t >= 1:
                        act.wait_ge(s["os_ps"], t)
                    act.copy(nv, heads(bank[7])).then_inc(s["nw_out"], 1)
                elif kind == "vn":
                    act.wait_ge(s["vn_ps"], t + 1)
                    act.copy(nv, heads(bank[3])).then_inc(s["vn_out"], 1)
                elif kind == "os":
                    act.wait_ge(s["os_ps"], t + 1)
                    act.copy(og[:, t], bank[3]).then_inc(s["os_out"], 1)

            for t in range(NT):
                act.wait_ge(s["mixT_ps"], t + 1)
                for a, gain in enumerate((sgc[:, 2:3], ggc[:])):
                    ins = act.activation(mixT[:, t, 4 * a:4 * a + 4], bank[2 * (t % 2) + a].rearrange("p (c i) -> p c i", c=4),
                                         ACT.Copy, scale=gain)
                ins.then_inc(s["mixT_out"], 1)

            def turned_h2(t):
                act.wait_ge(s["h2T_ps"], t + 1)
                act.copy(h2T, psum[:, 0:2].rearrange("p a (b i) -> p (a b) i", i=P)).then_inc(s["h2T_out"], 1)

            def queries(t):
                act.wait_ge(s["q_ps"], t + 1)
                act.copy(qs, psum[:, 0:4].rearrange("p a (b i) -> p (a b) i", i=P)).then_inc(s["q_out"], 1)

            def soft(group, where, h0, h1):
                c = slice(h0 * TOPK, h1 * TOPK)
                act.wait_ge(s["best_rdy"], group + 1)
                act.activation(where[:, c], where[:, c], ACT.Exp).then_inc(s["e_out"], 1)

            def diagonal(row, c):
                act.wait_ge(s["v_free"], SEL + row + c - VB + 1)
                act.activation(diag[c % VB], ident[:], ACT.Copy, scale=wt[:, c:c + 1]).then_inc(s["diag_rdy"], 1)

            def finish(i):
                act.wait_ge(s["w_rdy"], i * PH + PH)
                for c in range((PH - 1) * TOPK, SEL):
                    diagonal(i * SEL, c)
                act.wait_ge(s["v_free"], SEL + i * SEL + SEL)
                act.wait_ge(s["stored"], 16 * (i + 1))
                for half in range(2):
                    ins = act.copy(y_s[:, half * 512:(half + 1) * 512], bank[6 + half])
                ins.then_inc(s["y_out"], 1)

            turned_h2(0)
            queries(0)
            soft(0, gates, 0, EARLY)

            def tile(i):
                act.wait_ge(s["u_free"], i * SEL + UB)
                for half in range(2):
                    ins = act.copy(bank[4 + half], h2[:, half * 512:(half + 1) * 512])
                ins.then_inc(s["h2p_rdy"], 1)
                for h in range(PH):
                    if h >= 1:
                        act.wait_ge(s["w_rdy"], i * PH + h)
                        if is_first(i) and h == 1:
                            act.wait_ge(s["wo_ps"], 2 * NT)
                        for c in range((h - 1) * TOPK, h * TOPK):
                            if c == TURN_AT and not is_last(i):
                                turned_h2(i + 1)
                            if c == SCORE_AT and not is_last(i):
                                queries(i + 1)
                            if c == EXP_AT and not is_last(i):
                                soft(len(GROUPS0) + i, gates_n, 0, PH)
                            for group, (h0, h1, row, _) in enumerate(GROUPS0):
                                if is_first(i) and c == row:
                                    soft(group, gates, h0, h1)
                            diagonal(i * SEL, c)
                    elif not is_first(i):
                        finish(i - 1)
                    c = slice(h * TOPK, (h + 1) * TOPK)
                    act.wait_ge(s["dots_rdy"], i * PH + h + 1)
                    act.activation(gel[:, c], dots[:, c], ACT.Gelu).then_inc(s["gel_rdy"], 1)

            tiles(act, tile)
            finish(NT - 1)

        @block.vector
        def _(dve):
            def rsqrt(dst, v, n, add):
                t = st[:, 2, 0:dst.shape[-1]]
                w = st[:, 1, 0:dst.shape[-1]]
                dve.tensor_scalar(w, v, n, add, ALU.mult, ALU.add)
                dve.drain()
                dve.tensor_scalar(dst.bitcast(I32), w.bitcast(I32), 1, None, ALU.arith_shift_right)
                dve.drain()
                dve.tensor_scalar(dst.bitcast(I32), dst.bitcast(I32), -1.0, float(0x5F3759DF), ALU.mult, ALU.add)
                dve.drain()
                for _ in range(3):
                    dve.tensor_tensor(t, dst, dst, ALU.mult)
                    dve.drain()
                    dve.scalar_tensor_tensor(t, t, -0.5, w, ALU.mult, ALU.mult)
                    dve.drain()
                    dve.scalar_tensor_tensor(dst, t, 1.5, dst, ALU.add, ALU.mult)
                    dve.drain()

            def norm_rows(v, heads_, width, n, add, extra, tmp):
                k = v.shape[1] * heads_
                vv = v.rearrange("p t (h d) -> p (t h) d", h=heads_)
                sv = tmp[:, 0:k * width].rearrange("p (k d) -> p k d", k=k)
                dve.drain()
                dve.tensor_tensor(sv, vv, vv, ALU.mult)
                dve.drain()
                ss, rs = st[:, 3, 0:k], st[:, 0, 0:k]
                dve.tensor_reduce(ss, sv, AX.X, ALU.add)
                dve.drain()
                rsqrt(rs, ss, n, add)
                if extra != 1.0:
                    dve.tensor_scalar(rs, rs, extra, None, ALU.mult)
                    dve.drain()
                return dve.tensor_tensor(vv, vv, rs.unsqueeze(2).to_broadcast([P, k, width]), ALU.mult)

            dve.wait_ge(s["x_in"], 16)
            for t in range(NT):
                dve.tensor_tensor_reduce(xn[:, t], xs[:, t], xs[:, t], 1.0, 0.0, ALU.mult, ALU.add, st[:, 3, t:t + 1])
            dve.drain()
            rsqrt(st[:, 0, 0:NT], st[:, 3, 0:NT], 1.0 / D, EPS)
            for t in range(NT):
                dve.tensor_scalar(xn[:, t], xs[:, t], st[:, 0, t:t + 1], None, ALU.mult).then_inc(s["xn_rdy"], 1)
            dve.wait_ge(s["par_in"], 16 * NPAR)
            for dc in range(DC):
                dve.wait_ge(s["xT_ps"], dc + 1)
                dve.tensor_scalar(hT[:, dc], bank[4 + dc % 2][:], g1c[:, dc:dc + 1], None, ALU.mult).then_inc(s["hT_rdy"], 1)
            for r in raw:
                ins = dve.memset(r[:, 0:CONV - 1], 0.0)
            ins.then_inc(s["raw_clear"], 1)
            dve.wait_ge(s["ab_ps"], 1)
            dve.tensor_copy(ab[:], bank[7][:, 0:NT * 2 * GH].rearrange("p (t c) -> p t c", t=NT)).then_inc(s["ab_rdy"], 1)

            def conv_unit(i):
                dve.wait_ge(s["proj_out"], i + 1)
                if i >= 2:
                    dve.wait_ge(s["silu_done"], i - 1)
                b, h = divmod(i, GH)
                r, c, w = raw[i % 2], conv[i % 2], cwc[:, ("gq", "gk", "gv").index(BLOCKS[b]) * GH + h]
                dve.tensor_scalar(c, r[:, 0:T], w[:, 0:1], None, ALU.mult)
                for j in range(1, CONV):
                    dve.drain()
                    ins = dve.scalar_tensor_tensor(c, r[:, j:j + T], w[:, j:j + 1], c, ALU.mult, ALU.add)
                ins.then_inc(s["conv_done"], 1)

            dve.drain()
            dve.tensor_tensor(gt1, ab[:, :, 0:GH], abc[:, GH:].unsqueeze(1).to_broadcast([P, NT, GH]), ALU.add)
            dve.drain()
            dve.scalar_tensor_tensor(gt2, gt1, -1.0, gt1, ALU.mult, ALU.min).then_inc(s["gate_dve"], 1)
            dve.wait_ge(s["gate_act"], 2)
            dve.scalar_tensor_tensor(gt1, gt1, 0.0, gt2, ALU.max, ALU.add)
            dve.tensor_scalar(gt3, gt3, 1.0, None, ALU.add)
            nea = st[:, 3, 5 * GH:6 * GH]
            dve.tensor_scalar(nea, st[:, 3, 4 * GH:5 * GH], -1.0, None, ALU.mult)
            dve.drain()
            dve.reciprocal(beta, gt3)
            dve.tensor_tensor(g_, gt1, nea.unsqueeze(1).to_broadcast([P, NT, GH]), ALU.mult).then_inc(s["gate_dve"], 1)
            dve.wait_ge(s["gate_act"], 3)
            dve.scalar_tensor_tensor(nbe, egc, -1.0, beta, ALU.mult, ALU.mult).then_inc(s["gate_dve"], 1)
            dve.drain()
            dve.engine_nop().then_inc(s["gate_dve"], 1)

            def softplus_head(h):
                dve.wait_ge(s["l_rdy"], h + 1)
                if h >= 1:
                    dve.wait_ge(s["r_ps"], 3 * h)
                dve.scalar_tensor_tensor(sp_, zs[h % 2], 0.0, ez, ALU.max, ALU.add).then_inc(s["sp_rdy"], 1)

            def projected(p):
                if p < 3 * GH:
                    conv_unit(p)
                if p in (6, 10):
                    j = (p - 6) // 4
                    dve.wait_ge(s["tr_out"], TR.index(("fwd", 4 * j + 3, 0)) + 1)
                    norm_rows(tok[BLOCKS[j]], GH, GD, 1.0, EPS, GD ** -0.5 if j else 1.0, squares).then_inc(s["gnorm"], 1)
                b, u = divmod(p, 4)
                if BLOCKS[b] in ("sq", "sk"):
                    dve.wait_ge(s["proj_out"], p + 1)
                    norm_rows(tok[BLOCKS[b]][:, u:u + 1], SBH, SBD, 1.0 / SBD, EPS, SBD ** -0.5 if BLOCKS[b] == "sq" else 1.0,
                              squares).then_inc(s["snorm"], 1)

            def out_norm(t):
                dve.wait_ge(s["os_out"], t + 1)
                norm_rows(og[:, t:t + 1], GH, GD, 1.0 / GD, EPS, 1.0, squares_b)
                dve.drain()
                return dve.tensor_tensor(og[:, t], og[:, t], tok["z"][:, t], ALU.mult)

            for kind, t, i in ORDER:
                n = t * NL + i
                if kind == "proj":
                    if i == 1:
                        projected(t)
                elif kind == "fwd" and t == 3 * GH - 1:
                    dve.wait_ge(s["tr_ps"], TR.index(("fwd", t, 0)) + 1)
                    dve.memset(S, 0.0).then_inc(s["s_rdy"], 1)
                    dve.engine_nop().then_inc(s["raw_free"], 1)
                elif kind == "z":
                    h, m = t, 3 * t + i
                    off, width, _ = PARTS[i]
                    dve.wait_ge(s["z_ps"], m + 1)
                    if i == 0 and h >= 2:
                        dve.wait_ge(s["wt_rdy"], h - 1)
                    dve.tensor_tensor(zs[h % 2][:, off:off + width], bank[0][:, 0:width],
                                      sb_mask[:, off:off + width], ALU.add).then_inc(s["z_out"], 1)
                    if i == 2:
                        dve.drain()
                        dve.scalar_tensor_tensor(ez, zs[h % 2], -1.0, zs[h % 2], ALU.mult, ALU.min).then_inc(s["nabs_rdy"], 1)
                        if h == 0:
                            softplus_head(0)
                elif kind == "r":
                    h, m = t, 3 * t + i
                    off, width, _ = PARTS[i]
                    dve.wait_ge(s["r_ps"], m + 1)
                    z = zs[h % 2][:, off:off + width]
                    dve.tensor_tensor(z, z, bank[1][:, 0:width], ALU.subtract).then_inc(s["arg_rdy"], 1)
                    if i == 2 and h + 1 < SBH:
                        softplus_head(h + 1)
                elif kind == "bc":
                    dve.wait_ge(s["qd_rdy"], t + 1)
                    dve.drain()
                    dve.tensor_tensor(decT, heads(bank[4]), causal_add[:].unsqueeze(1).to_broadcast([P, GH, P]), ALU.add).then_inc(s["arg_g"], 1)
                    dve.wait_ge(s["tr_out"], TR.index(("gback", 3, 0)) + 1)
                    dve.tensor_tensor(kbT, gkT[:, :, t * P:(t + 1) * P], heads(bank[5]), ALU.mult).then_inc(s["kb_rdy"], 1)
                elif kind == "kk":
                    dve.wait_ge(s["kk_ps"], t + 1)
                    dve.wait_ge(s["dec_rdy"], t + 1)
                    if t >= 1:
                        dve.wait_ge(s["ats_rdy"], NL * t)
                    dve.tensor_tensor(AT, heads(bank[6]), decT, ALU.mult).then_inc(s["at_rdy"], 1)
                elif kind == "qk":
                    dve.wait_ge(s["qk_ps"], t + 1)
                    if t >= 2:
                        dve.wait_ge(s["os_ps"], t - 1)
                    dve.tensor_tensor(qdT[t % 2], qdT[t % 2], gqT[:, :, t * P:(t + 1) * P], ALU.mult)
                    dve.tensor_tensor(attnT[t % 2], heads(bank[7]), decT, ALU.mult)
                    dve.drain()
                    dve.engine_nop().then_inc(s["attn_rdy"], 1)
                elif kind == "y":
                    dve.wait_ge(s["y_ps"], n + 1)
                    if i == 0 and t >= 2:
                        dve.wait_ge(s["vn_ps"], t - 1)
                    dve.drain()
                    idb = ident[:].unsqueeze(1).to_broadcast([P, GH, P])
                    tt = TTI[t % 2]
                    if i < NL - 1:
                        dve.tensor_tensor(TI, TI if i else idb, heads(bank[5]), ALU.subtract).then_inc(s["ti_rdy"], 1)
                    else:
                        dve.engine_nop().then_inc(s["ti_rdy"], 1)
                    dve.tensor_tensor(tt, tt if i else idb, heads(bank[6]), ALU.subtract).then_inc(s["ti_rdy"], 1)
                elif kind == "nw" and t >= 1:
                    out_norm(t - 1)
                elif kind == "os":
                    dve.wait_ge(s["os_ps"], t + 1)
                    dve.drain()
                    dve.tensor_tensor(S, S, etot[:, t].unsqueeze(2).to_broadcast([P, GH, P]), ALU.mult)
                    dve.drain()
                    dve.tensor_tensor(S, S, heads(bank[7]), ALU.add).then_inc(s["s_rdy"], 1)

            dve.wait_ge(s["o_out"], SBH)
            norm_rows(osb[:, 0:1], SBH, SBD, 1.0 / SBD, EPS, 1.0, squares_b).then_inc(s["mix_rdy"], 1)
            out_norm(NT - 1).then_inc(s["mix_rdy"], 1)
            norm_rows(osb[:, 1:], SBH, SBD, 1.0 / SBD, EPS, 1.0, squares_c).then_inc(s["mix_rdy"], 1)

            def residual(n):
                t, half = divmod(n, 2)
                dve.wait_ge(s["wo_ps"], n + 1)
                xv = xs[:, t, half * 512:(half + 1) * 512]
                dve.tensor_tensor(xv, xv, bank[wo_bank(n)], ALU.add).then_inc(s["x2_rdy"], 1)

            residual(0)
            residual(1)

            dve.engine_nop().then_inc(s["u_free"], UB)
            dve.engine_nop().then_inc(s["v_free"], SEL)
            dve.engine_nop().then_inc(s["y_out"], 1)
            dve.engine_nop().then_inc(s["stored"], 16)
            idb16 = iota[:].unsqueeze(1).to_broadcast([P, TOPK, TOPK])

            def top16(out, idx, vals, left):
                for o, i_, v, l_ in zip(out, idx, vals, left):
                    dve.max(o[:, 0:8], v)
                dve.drain()
                for o, i_, v, l_ in zip(out, idx, vals, left):
                    dve.max_index(i_[:, 0:8], o[:, 0:8], v)
                    dve.match_replace(l_, o[:, 0:8], v, LOWEST)
                dve.drain()
                for o, i_, v, l_ in zip(out, idx, vals, left):
                    dve.max(o[:, 8:16], l_)
                dve.drain()
                for o, i_, v, l_ in zip(out, idx, vals, left):
                    ins = dve.max_index(i_[:, 8:16], o[:, 8:16], l_)
                return ins

            def norm2(t):
                xt = x2[:, bass.ds(t * D, D)]
                if not is_first(t):
                    by_itself(dve, s["h2T_ps"], t)
                dve.drain()
                dve.tensor_tensor(h2sq, xt, xt, ALU.mult)
                dve.drain()
                dve.tensor_reduce(st[:, 3, 0:1], h2sq, AX.X, ALU.add)
                dve.drain()
                rsqrt(st[:, 0, 0:1], st[:, 3, 0:1], 1.0 / D, EPS)
                dve.scalar_tensor_tensor(h2, xt, st[:, 0, 0:1], g2b, ALU.mult, ALU.mult).then_inc(s["h2_rdy"], 1)

            def choose(t, h, into_id, into_gate, signal):
                c = slice(h * TOPK, (h + 1) * TOPK)
                by_itself(dve, s["sc_ps"], t + 1)
                dve.drain()
                sc_ = [bank[(2 * h + a) // 4][:, ((2 * h + a) % 4) * NKEYS:((2 * h + a) % 4 + 1) * NKEYS] for a in range(2)]
                top16([top[:, 0], top[:, 1]], [topi[:, 0], topi[:, 1]], sc_, [rest[:, 0], rest[:, 1]])
                dve.drain()
                dve.engine_nop().then_inc(s["picked"], 1)
                dve.tensor_tensor(cand.rearrange("p (a b) -> p a b", a=TOPK), top[:, 0].unsqueeze(2).to_broadcast([P, TOPK, TOPK]),
                                  top[:, 1].unsqueeze(1).to_broadcast([P, TOPK, TOPK]), ALU.add)
                dve.drain()
                top16([best], [pos], [cand], [crest])
                dve.drain()
                ins = dve.tensor_scalar(into_gate[:, c], best, best[:, 0:1], None, ALU.subtract)
                if signal:
                    ins.then_inc(s["best_rdy"], 1)
                dve.tensor_scalar(pos1, pos, 4, None, ALU.logical_shift_right)
                dve.tensor_scalar(pos2, pos, TOPK - 1, None, ALU.bitwise_and)
                dve.drain()
                for e, q in ((eq1, pos1), (eq2, pos2)):
                    dve.tensor_tensor(e, q.unsqueeze(2).to_broadcast([P, TOPK, TOPK]), idb16, ALU.is_equal)
                dve.drain()
                for e, a in ((eq1, 0), (eq2, 1)):
                    dve.tensor_tensor(e, e, topi[:, a].unsqueeze(1).to_broadcast([P, TOPK, TOPK]), ALU.mult)
                dve.drain()
                dve.tensor_reduce(id1, eq1, AX.X, ALU.add)
                dve.tensor_reduce(id2, eq2, AX.X, ALU.add)
                dve.drain()
                ins = dve.scalar_tensor_tensor(into_id[:, c], id1, float(NKEYS), id2, ALU.mult, ALU.add)
                if is_first(t):
                    ins.then_inc(s["eid_rdy"], 1)

            def soften(group, src, h0, h1):
                k = h1 - h0
                c = slice(h0 * TOPK, h1 * TOPK)
                src, dst = (v[:, c].rearrange("p (h k) -> p h k", h=k) for v in (src, gates))
                by_itself(dve, s["e_out"], group + 1)
                dve.tensor_reduce(esum[:, 0:k], src, AX.X, ALU.add)
                dve.drain()
                dve.reciprocal(erec[:, 0:k], esum[:, 0:k])
                dve.drain()
                dve.tensor_tensor(dst, src, erec[:, 0:k].unsqueeze(2).to_broadcast([P, k, TOPK]), ALU.mult)

            def take(h0, h1):
                c = slice(h0 * TOPK, h1 * TOPK)
                dve.drain()
                dve.tensor_copy(eid[:, c], eid_n[:, c]).then_inc(s["eid_rdy"], h1 - h0)

            x2 = xs.rearrange("p t d -> p (t d)")
            dve.wait_ge(s["g2_in"], 16)
            norm2(0)
            residual(2)
            for h in range(EARLY):
                choose(0, h, eid, gates, h == EARLY - 1)
            soften(0, gates, 0, EARLY)

            def tile(i):
                for h in range(PH):
                    if h == 0:
                        dve.wait_ge(s["h2p_rdy"], i + 1)
                    for k in range(TOPK):
                        c = h * TOPK + k
                        if is_first(i) and c in (0, 3, 8, 11, 14):
                            residual(3 + (0, 3, 8, 11, 14).index(c))
                        by_itself(dve, u_in[c % UB], 16 * (i * (SEL // UB) + c // UB + 1))
                        dve.tensor_tensor_reduce(u_row[c % UB], u_row[c % UB], h2p, 1.0, 0.0, ALU.mult, ALU.add,
                                                 dots[:, c:c + 1]).then_inc(s["u_free"], 1)
                        if chosen_after(i, c):
                            who, head = chosen_after(i, c)
                            last = head in ([PH - 1] if who else [h1 - 1 for _, h1, _, _ in GROUPS0])
                            choose(i + who, head, *((eid_n, gates_n) if who else (eid, gates)), last)
                    dve.drain()
                    dve.engine_nop().then_inc(s["dots_rdy"], 1)
                    for group, (h0, h1, _, before) in enumerate(GROUPS0):
                        if is_first(i) and h == before:
                            soften(group, gates, h0, h1)
                    if h == 0 and not is_first(i):
                        soften(len(GROUPS0) + i - 1, gates_n, 0, PH)
                    c = slice(h * TOPK, (h + 1) * TOPK)
                    by_itself(dve, s["gel_rdy"], i * PH + h + 1)
                    dve.drain()
                    dve.tensor_tensor(wt[:, c], gel[:, c], gates[:, c], ALU.mult).then_inc(s["w_rdy"], 1)
                    if h == 1 and not is_first(i):
                        by_itself(dve, s["v_free"], SEL + i * SEL)
                        take(PH - 2, PH)
                    if h == 2 and not is_last(i):
                        norm2(i + 1)
                if not is_last(i):
                    by_itself(dve, s["v_free"], SEL + i * SEL + (PH - 2) * TOPK)
                    take(0, PH - 2)

            tiles(dve, tile)



_OUTS = ((1, T, D), "float32")


def kernel(**inputs):
    import numpy as _np
    import concourse.bacc as _bacc
    from concourse import mybir as _mybir
    from concourse.bass_utils import run_bass_kernel_spmd as _run

    a = {k: _np.asarray(v) for k, v in inputs.items()}
    a["norm1_g"] = a["norm1_g"][0].reshape(DC, P).T
    a["gdn_conv_w"] = a["gdn_conv_w"][0].reshape(CONV, 3 * GH, P).transpose(2, 1, 0)
    keys = _np.stack([a.pop("peer_keys1")[0], a.pop("peer_keys2")[0]], 1)
    a["keys_t"] = keys.reshape(1, NS, NKEYS, HALF).transpose(0, 1, 3, 2)

    nc = _bacc.Bacc("TRN2", target_bir_lowering=False, num_devices=1)
    arrays, args = {}, []
    for name in ("x", "norm1_g", "w_in", "sb_q_norm_g", "sb_k_norm_g", "sb_out_norm_g", "gdn_conv_w", "gdn_a_log",
                 "gdn_dt_bias", "gdn_out_norm_g", "w_out", "norm2_g", "peer_w_q", "keys_t", "peer_u", "peer_v"):
        v = _np.ascontiguousarray(a[name])
        arrays[f"in_{name}"] = v
        args.append(nc.dram_tensor(f"in_{name}", v.shape, _mybir.dt.from_np(v.dtype), kind="ExternalInput").ap())
    out = nc.dram_tensor("out_0", _OUTS[0], _mybir.dt.from_np(_np.dtype(_OUTS[1])), kind="ExternalOutput").ap()
    layer_kernel(nc, *args, out)
    r = _run(nc, [arrays], core_ids=[0])
    return r.results[0]["out_0"]
```

```python
import math
from contextlib import ExitStack

import concourse.bass as bass
from concourse import mybir

ALU = mybir.AluOpType
ACT = mybir.ActivationFunctionType
AX = mybir.AxisListType
F32 = mybir.dt.float32
I32 = mybir.dt.int32
U32 = mybir.dt.uint32

P = 128
D = 1024
T = 512
NT = T // P
DC = D // P
SBH, SBD = 8, 64
SBW = SBH * SBD
GH, GD = 4, 128
GW = GH * GD
CONV = 4
EPS = 1e-6
COL_GQ, COL_Z = 3 * SBW, 3 * SBW + 3 * GW
COL_AB = COL_Z + GW
PH, NKEYS, HALF, TOPK = 8, 128, 128, 16
NS = 2 * PH
SEL = PH * TOPK
NEG = -1.0e30
LOWEST = -3.0e38
LEVELS = [1 << i for i in range(7)]

KB_ORDER = [0, 1, 3, 2]
KB_OFF, _o = {}, 0
for _kb in KB_ORDER:
    KB_OFF[_kb] = _o
    _o += T - P * _kb
RAG = _o
PARTS = [(0, 512, [0]), (512, 512, [1, 3]), (1024, 256, [2])]

KB = 256

BLOCKS = ["gk", "gq", "gv", "z", "sq", "sk", "sv"]
BLOCK_COL = {"gq": COL_GQ, "gk": COL_GQ + GW, "gv": COL_GQ + 2 * GW, "z": COL_Z,
             "sq": 0, "sk": SBW, "sv": 2 * SBW}
NUNIT = 4 * len(BLOCKS)
NL = len(LEVELS)
NPAR = 4 + 6 + 1


def spread(main, extra):
    out, j = [], 0
    for i, m in enumerate(main):
        out.append(m)
        want = len(extra) * (i + 1) // len(main)
        out += extra[j:want]
        j = want
    return out


def stage_ab_order():
    proj = []
    for p in range(NUNIT):
        proj += [("proj", p, 0), ("proj", p, 1)]
        if 3 <= p < 8:
            proj.append(("gate", p - 3, 0))
        if 2 <= p < 14:
            proj.append(("fwd", p - 2, 0))
        if 10 <= p < 14:
            proj.append(("gback", p - 10, 0))
        if 14 <= p < 18:
            proj.append(("gback", p - 10, 0))
        if 21 <= p < 25:
            proj.append(("sback", p - 21, 0))
        if p >= 25:
            proj.append(("sback", p - 21, 0))
    proj.append(("sback", 7, 0))

    def inverse(t, rec):
        head = [("bc", t, 0), ("kk", t, 0)] + ([("qk", t, 0)] if t else [])
        levels = [(k, t, lv) for lv in range(NL) for k in ("x", "y")]
        return head + spread(levels, rec)

    def recur(t):
        return [("mul", t, 0), ("nw", t, 0), ("vn", t, 0), ("os", t, 0)]

    gdn = inverse(0, []) + [("qk", 0, 0)]
    for t in range(1, NT):
        gdn += inverse(t, recur(t - 1))
    gdn += recur(NT - 1)

    first = proj.index(("proj", 14, 0))
    late = proj[first:]
    out, j, rest = proj[:first], 0, False
    for step in late:
        out.append(step)
        if step[0] == "proj":
            if not rest:
                out.append(gdn[j])
                j += 1
            rest = not rest and gdn[j - 1][0] == "y"
    sb = []
    for h in range(SBH + 2):
        zz = [("z", h, i) for i in range(3)] if h < SBH else []
        rr = [("r", h - 1, i) for i in range(3)] if 1 <= h <= SBH else []
        oo = [("o", h - 2, 0)] if h >= 2 else []
        sb += zz[:2] + rr[:1] + zz[2:] + rr[1:2] + oo + rr[2:]
    return out + spread(gdn[j:], sb)


def layer_kernel(nc, x, norm1_g, w_in, sb_q_norm_g, sb_k_norm_g, sb_out_norm_g, gdn_conv_w, gdn_a_log,
                 gdn_dt_bias, gdn_out_norm_g, w_out, norm2_g, peer_w_q, keys_t, peer_u, peer_v, out):
    x_d = x[0].rearrange("(t p) d -> p t d", p=P)
    out_d = out[0].rearrange("(t p) d -> p t d", p=P)
    w_in_d = w_in[0].rearrange("(c p) n -> p c n", p=P)
    w_out_d = w_out[0].rearrange("(c p) n -> p c n", p=P)
    w_q_d = peer_w_q[0].rearrange("(c p) n -> p c n", p=P)
    u_d, v_d = peer_u[0], peer_v[0]

    with ExitStack() as ctx:
        def sb(name, shape, dt=F32):
            return ctx.enter_context(nc.sbuf_tensor(name, shape, dt))

        def sem(name):
            return ctx.enter_context(nc.semaphore(name))

        arena = sb("arena", [P, 203 * KB])

        def at(kb, *shape):
            n = math.prod(shape)
            o = int(kb * KB)
            v = arena[:, o:o + n]
            if len(shape) == 2:
                v = v.rearrange("p (a b) -> p a b", a=shape[0])
            elif len(shape) == 3:
                v = v.rearrange("p (a b c) -> p a b c", a=shape[0], b=shape[1])
            return v

        xs = at(0, NT, D)
        hT = at(16, DC, T)
        wbuf = [at(32 + 16 * i, DC, 512) for i in range(2)]
        wab = at(80, DC, 2 * GH)
        abT = at(82, T)[0:2 * GH]
        tok = {"gq": at(80, NT, GW), "gk": at(88, NT, GW), "gv": at(96, NT, GW), "z": at(120, NT, GW),
               "sq": at(136, NT, SBW), "sk": at(128, NT, SBW), "sv": at(144, NT, SBW)}
        gqT, gkT = at(104, GH, T), at(112, GH, T)
        sqT, skT = at(152, SBH // 2, T), at(160, SBH // 2, T)
        xn = at(168, NT, D)
        raw = [at(168 + 2.25 * i, T + CONV - 1) for i in range(2)]
        conv = [at(173 + 2 * i, T) for i in range(2)]
        act_o = [at(177 + 2 * i, T) for i in range(2)]
        squares = at(182, NT * GW)
        sb_mask = at(190, RAG)
        lv_mask = at(195, NL, P)
        decT, kbT, AT, TI, ATs0, ATs1, XW, TT0 = (at(64 + 2 * i, GH, P) for i in range(8))
        ATs = [ATs0, ATs1]
        TT1, S, qd0, qd1, at0, at1 = (at(168 + 2 * i, GH, P) for i in range(6))
        TTI, qdT, attnT = [TT0, TT1], [qd0, qd1], [at0, at1]
        kd, nv = at(199, GW), at(201, GH, P)
        vb, kbe, og, osb = tok["gv"], tok["gk"], tok["gq"], tok["sq"]
        zs = [at(16 + 5 * i, RAG) for i in range(2)]
        ez, sp_ = at(26, RAG), at(31, RAG)
        wts = [at(36 + 5 * i, RAG) for i in range(2)]
        squares_b = at(62, GW)
        w_out_s = [at(k, D) for k in (46, 50, 54, 58, 128, 132, 182, 186)]
        mixT = at(16, NT, DC, P)
        squares_c = at(20, (NT - 1) * SBW)
        w_q_s = [at(k, NS * HALF) for k in (104, 112, 152, 160, 88, 96, 144, 120)]
        keysT = at(168, NS, NKEYS)
        UB, VB = 8, 8
        u_row = [at(k, D) for k in (36, 40, 64, 68, 72, 76, 80, 84)]
        v_row = [at(k, D) for k in (16, 20, 24, 28, 46, 50, 54, 58)]
        g2b = at(32, D)
        eid, eid_n = (at(44 + 0.5 * i, SEL).bitcast(U32) for i in range(2))
        gates, gates_n = (at(45 + 0.5 * i, SEL) for i in range(2))
        dots, gel, wt = (at(180 + 0.5 * i, SEL) for i in range(3))
        y_s = at(128, D)
        diag = [at(132 + 0.5 * i, P) for i in range(VB)]
        qs = at(190, NS, P)
        h2sq = at(190, D)
        h2 = at(176, D)
        h2T = at(199, DC, P)
        top = at(136, 2, TOPK)
        topi = at(136.25, 2, TOPK).bitcast(U32)
        rest = at(137, 2, NKEYS)
        cand, crest = at(138, TOPK * TOPK), at(139, TOPK * TOPK)
        eq1, eq2 = at(140, TOPK, TOPK), at(141, TOPK, TOPK)
        best, id1, id2, esum, erec = (at(142 + i * 0.0625, TOPK) for i in range(5))
        pos, pos1, pos2 = (at(143 + i * 0.0625, TOPK).bitcast(U32) for i in range(3))

        iota = sb("iota", [P, TOPK])
        ident = sb("ident", [P, P])
        ones = sb("ones", [P, P])
        tri_ge = sb("tri_ge", [P, P])
        tri_gt = sb("tri_gt", [P, P])
        tri_le = sb("tri_le", [P, P])
        causal_add = sb("causal_add", [P, P])
        g1c = sb("g1c", [P, DC])
        sgc = sb("sgc", [P, 3])
        ggc = sb("ggc", [P, 1])
        cwc = sb("cwc", [P, 3 * GH, CONV])
        abc = sb("abc", [P, 2 * GH])
        g_rs = sb("g_rs", [P, 2, NT * GH])
        st = sb("st", [P, 4, 32])
        ab = sb("ab", [P, NT, 2 * GH])
        gt = sb("gt", [P, 10, NT, GH])
        g_, beta, ngc, egc, nbe, ekd, etot, gt1, gt2, gt3 = (gt[:, i] for i in range(10))

        psum = ctx.enter_context(nc.psum_tensor("psum", [P, 8, 512], F32))
        bank = [psum[:, i] for i in range(8)]

        u_in = [sem(f"u_in{i}") for i in range(UB)]
        v_in = [sem(f"v_in{i}") for i in range(VB)]
        s = {n: sem(n) for n in (
            "y_out", "stored", "dve_turns", "pool_turns", "sc_ps", "picked", "best_rdy", "e_out", "eid_rdy", "u_free", "v_free",
            "h2p_rdy", "gel_rdy", "dots_rdy", "w_rdy", "diag_rdy",
            "sq_rdy", "rs_rdy", "x0_in", "x1_in", "x2_in", "x3_in", "x_scale", "par_in", "w0_in", "w1_in", "wab_in", "wout_in", "wq_in", "keys_in", "g2_in",
            "consts", "xn_rdy", "xT_ps", "hT_rdy", "ab_ps", "ab_rdy",
            "proj_ps", "proj_out", "conv_done", "silu_done", "tr_ps", "tr_out", "gnorm", "snorm",
            "raw_clear", "raw_free", "gate_dve", "gate_act", "gate_ps", "mul_rdy", "qk_ps", "attn_rdy",
            "z_ps", "z_out", "nabs_rdy", "e_rdy", "l_rdy", "sp_rdy", "r_ps", "arg_rdy", "wt_rdy",
            "o_ps", "o_out",
            "bc_ps", "arg_g", "dec_rdy", "kb_rdy", "qd_rdy", "kk_ps", "at_rdy", "ats_rdy",
            "x_ps", "x_out", "y_ps", "ti_rdy", "nw_ps", "nw_out", "vn_ps", "vn_out", "os_ps", "os_out",
            "s_rdy", "mix_rdy", "mixT_ps", "mixT_out", "wo_ps", "x2_rdy", "h2_rdy", "h2T_ps", "h2T_out",
            "q_ps", "q_out")}
        ORDER = stage_ab_order()
        TR = [step for step in ORDER if step[0] in ("fwd", "gback", "sback")]

        def count(kind, until):
            return sum(step[0] == kind for step in ORDER[:until])

        def heads(v):
            return v.rearrange("p (h i) -> p h i", h=GH)

        h2p = psum[:, 4:6].rearrange("p a b -> p (a b)")

        NORM_AT = [6, 10]

        def by_itself(eng, semaphore, value):
            eng.wait_ge(semaphore, value)
            eng.sem_inc(s["dve_turns" if eng is nc.vector else "pool_turns"], 1)

        def tiles(eng, body):
            body(0)
            with eng.Fori(1, NT - 1) as i:
                body(i)
            body(NT - 1)

        EARLY = 1
        AHEAD = 2
        FIRST_AT = [3, 22, 35, 38, 41, 44, 47]
        GROUPS0 = [(0, 1, None, None), (1, 3, None, 1), (3, 8, 33, 3)]
        RESIDUAL_AT = [14, 18, 21, 24, 28]
        TURN_AT, QUERY_AT = 2 * TOPK, 2 * TOPK + 4
        SCORE_AT = QUERY_AT + 2 * NS
        NEXT_AT = SCORE_AT + TOPK + 4
        TAKE_AT = NEXT_AT + 5 * (PH - 3) + 2
        EXP_AT = NEXT_AT + 5 * PH - 1 - TOPK

        def chosen_after(i, c):
            if is_first(i) and c in FIRST_AT:
                return 0, EARLY + FIRST_AT.index(c)
            n, left = divmod(c - NEXT_AT, 5)
            if not is_last(i) and n in range(PH) and left == 0:
                return 1, n
            return None

        def wo_bank(n):
            return 4 + n if n < 4 else 6 + n % 2

        def is_first(i):
            return isinstance(i, int) and i == 0

        def is_last(i):
            return isinstance(i, int) and i == NT - 1

        block = ctx.enter_context(nc.Block())

        @block.sync
        def _(sp):
            for t in range(NT):
                sp.dma_start(xs[:, t], x_d[:, t]).then_inc(s[f"x{t}_in"], 16)
            sp.dma_start(wbuf[0], w_in_d[:, :, BLOCK_COL[BLOCKS[0]]:BLOCK_COL[BLOCKS[0]] + 512]).then_inc(s["w0_in"], 16)
            sp.dma_start(wab, w_in_d[:, :, COL_AB:COL_AB + 2 * GH]).then_inc(s["wab_in"], 16)
            pars = [(g1c[:], norm1_g),
                    (ggc[:], gdn_out_norm_g[0].rearrange("(p o) -> p o", o=1)),
                    (abc[:, 0:GH], gdn_a_log[0].partition_broadcast(P)),
                    (abc[:, GH:2 * GH], gdn_dt_bias[0].partition_broadcast(P))]
            for i, g in enumerate((sb_q_norm_g, sb_k_norm_g, sb_out_norm_g)):
                for half in range(2):
                    pars.append((sgc[half * SBD:(half + 1) * SBD, i:i + 1],
                                 g[0].rearrange("(p o) -> p o", o=1)))
            pars.append((cwc[:], gdn_conv_w))
            assert len(pars) == NPAR
            for dst, src in pars:
                sp.dma_start(dst, src).then_inc(s["par_in"], 16)
            for b, name in list(enumerate(BLOCKS))[1:]:
                if b >= 2:
                    sp.wait_ge(s["proj_ps"], 4 * (b - 1))
                c0 = BLOCK_COL[name]
                sp.dma_start(wbuf[b % 2], w_in_d[:, :, c0:c0 + 512]).then_inc(s[f"w{b % 2}_in"], 16)
            sp.wait_ge(s["proj_ps"], NUNIT)
            sp.wait_ge(s["tr_ps"], len(TR))
            sp.wait_ge(s["snorm"], 2 * NT)
            for c in range(DC):
                sp.dma_start(w_out_s[c], w_out_d[:, c]).then_inc(s["wout_in"], 16)
            for c in range(DC):
                if c == 0:
                    sp.wait_ge(s["attn_rdy"], NT)
                elif c == 2:
                    sp.wait_ge(s["z_ps"], 3 * SBH)
                elif c == 4:
                    sp.wait_ge(s["vn_ps"], NT)
                elif c == 6:
                    sp.wait_ge(s["o_ps"], SBH)
                    sp.wait_ge(s["s_rdy"], NT + 1)
                    sp.dma_start(g2b, norm2_g[0].partition_broadcast(P)).then_inc(s["g2_in"], 16)
                    sp.dma_start(keysT, keys_t[0].rearrange("a d n -> d a n")).then_inc(s["keys_in"], 16)
                elif c == 7:
                    sp.wait_ge(s["mix_rdy"], 2)
                sp.dma_start(w_q_s[c], w_q_d[:, c]).then_inc(s["wq_in"], 16)
            with sp.Fori(0, NT) as i:
                sp.wait_ge(s["y_out"], i + 2)
                sp.dma_start(out_d[:, bass.ds(i, 1)].rearrange("p o d -> p (o d)"), y_s).then_inc(s["stored"], 16)
            sp.wait_ge(s["stored"], 16 * (NT + 1))

        @block.gpsimd
        def _(pool):
            pool.memset(ones[:], 1.0)
            pool.memset(sb_mask, 0.0)
            pool.memset(causal_add[:], 0.0)
            pool.memset(lv_mask, 1.0)
            pool.drain()

            def tri(dst, src, op, base, cm, step, fill):
                return pool.affine_select(out=dst, in_=src, compare_op=op, fill=fill, base=base,
                                          pattern=[[step, P]], channel_multiplier=cm)
            tri(ident[:], ones[:], ALU.is_equal, 0, 1, -1, 0.0)
            tri(tri_ge[:], ones[:], ALU.is_ge, 0, 1, -1, 0.0)
            tri(tri_gt[:], ones[:], ALU.is_gt, 0, 1, -1, 0.0)
            tri(tri_le[:], ones[:], ALU.is_ge, 0, -1, 1, 0.0)
            tri(causal_add[:], causal_add[:], ALU.is_ge, 0, -1, 1, NEG)
            for kb in range(NT):
                o = sb_mask[:, KB_OFF[kb]:KB_OFF[kb] + P]
                tri(o, o, ALU.is_gt, 0, -1, 1, NEG)
            for lv, z in enumerate(LEVELS):
                n = P // (2 * z)
                m = lv_mask[:, lv].rearrange("p (b h z) -> p b h z", b=n, h=2)
                pool.memset(m[:, :, 0], 0.0)
                pool.drain()
                pool.affine_select(out=m, in_=m, compare_op=ALU.is_ge, fill=0.0, base=0,
                                   pattern=[[-2 * z, n], [0, 2], [0, z]], channel_multiplier=1)
                pool.drain()
                last = pool.affine_select(out=m, in_=m, compare_op=ALU.is_ge, fill=0.0, base=z - 1,
                                          pattern=[[2 * z, n], [0, 2], [0, z]], channel_multiplier=-1)
            pool.iota(iota[:], pattern=[[1, TOPK]], base=0, channel_multiplier=0,
                      allow_small_or_imprecise_dtypes=True)
            pool.drain()
            pool.engine_nop().then_inc(s["consts"], 1)

            def level_mask(t, lv):
                n = t * NL + lv
                if lv == 0:
                    pool.wait_ge(s["at_rdy"], t + 1)
                if n >= 2:
                    pool.wait_ge(s["x_ps"], n - 1)
                if lv == 2:
                    pool.wait_ge(s["ti_rdy"], 2 * NL * t + 2)
                pool.tensor_tensor(ATs[n % 2], AT, lv_mask[:, lv].unsqueeze(1).to_broadcast([P, GH, P]),
                                   ALU.mult).then_inc(s["ats_rdy"], 1)

            def on_rows(dst, src, gate, t):
                return pool.tensor_tensor(heads(dst), heads(src), gate[:, t].unsqueeze(2).to_broadcast([P, GH, GD]),
                                          ALU.mult)

            for kind, t, i in ORDER:
                if kind == "proj" and i == 0 and t in NORM_AT:
                    j = NORM_AT.index(t)
                    pool.wait_ge(s["rs_rdy"], j + 1)
                    for tile_ in range(NT):
                        v = heads(tok[BLOCKS[j]][:, tile_])
                        pool.tensor_tensor(v, v, g_rs[:, j, tile_ * GH:(tile_ + 1) * GH].unsqueeze(2).to_broadcast([P, GH, GD]),
                                           ALU.mult).then_inc(s["gnorm"], 1)
                elif kind == "kk":
                    level_mask(t, 0)
                    level_mask(t, 1)
                elif kind == "x" and i + 2 < NL:
                    level_mask(t, i + 2)
                elif kind == "mul":
                    if t == 0:
                        pool.wait_ge(s["gate_dve"], 4)
                        pool.wait_ge(s["tr_out"], max(TR.index(("gback", 3, 0)), TR.index(("fwd", 11, 0))) + 1)
                        pool.wait_ge(s["raw_free"], 1)
                    else:
                        pool.wait_ge(s["os_ps"], t)
                    on_rows(kd, tok["gk"][:, t], ekd, t)
                    on_rows(vb[:, t], vb[:, t], beta, t)
                    pool.drain()
                    on_rows(kbe[:, t], kbe[:, t], nbe, t).then_inc(s["mul_rdy"], 1)

            def gather(buf, table, col, landed):
                pool.indirect_dma_start(buf, None, table, bass.IndirectOffsetOnAxis(ap=eid[:, col:col + 1], axis=0)
                                        ).then_inc(landed, 16)

            def gather_v(row, c):
                by_itself(pool, s["v_free"], SEL + row + c - VB + 1)
                gather(v_row[c % VB], v_d, c, v_in[c % VB])

            def tile(i):
                for h in range(PH):
                    by_itself(pool, s["eid_rdy"], i * PH + h + 1)
                    if is_first(i) and h == 2:
                        pool.wait_ge(s["wo_ps"], 2 * NT)
                    for k in range(TOPK):
                        c = h * TOPK + k
                        by_itself(pool, s["u_free"], i * SEL + c + 1)
                        gather(u_row[c % UB], u_d, c, u_in[c % UB])
                        if is_first(i) and h <= 2:
                            if h == 2:
                                gather_v(0, 2 * k)
                                gather_v(0, 2 * k + 1)
                        elif h >= 1:
                            gather_v(i * SEL, (h - 1) * TOPK + k)
                        else:
                            gather_v((i - 1) * SEL, (PH - 1) * TOPK + k)

            pool.wait_ge(s["mixT_ps"], NT)
            tiles(pool, tile)
            for k in range(TOPK):
                gather_v((NT - 1) * SEL, (PH - 1) * TOPK + k)

        @block.tensor
        def _(pe):
            pe.wait_ge(s["consts"], 1)
            for dc in range(DC):
                if dc == 0:
                    pe.wait_ge(s["xn_rdy"], NT)
                if dc >= 2:
                    pe.wait_ge(s["hT_rdy"], dc - 1)
                for t in range(NT):
                    mm = pe.transpose(bank[4 + dc % 2][:, t * P:(t + 1) * P], xn[:, t, dc * P:(dc + 1) * P], ident[:])
                mm.then_inc(s["xT_ps"], 1)
            def gate_steps(step):
                if step == 0:
                    pe.wait_ge(s["wab_in"], 16)
                    for dc in range(DC):
                        mm = pe.matmul(bank[7][0:2 * GH], wab[:, dc], hT[:, dc], start=dc == 0, stop=dc == DC - 1)
                    mm.then_inc(s["ab_ps"], 1)
                elif step == 1:
                    pe.wait_ge(s["ab_rdy"], 1)
                    for t in range(NT):
                        mm = pe.transpose(bank[7][:, t * 2 * GH:(t + 1) * 2 * GH], abT[:, t * P:(t + 1) * P],
                                          ident[0:2 * GH, 0:2 * GH])
                    mm.then_inc(s["ab_ps"], 1)
                elif step == 3:
                    pe.wait_ge(s["gate_dve"], 2)
                    gall = g_.rearrange("p t h -> p (t h)")
                    pe.matmul(bank[3][:, 0:16], tri_le[:], gall, start=True, stop=True)
                    pe.matmul(bank[3][:, 16:32], tri_gt[:], gall, start=True, stop=True)
                    pe.matmul(bank[3][:, 32:48], ones[:], gall, start=True, stop=True).then_inc(s["gate_ps"], 1)

            def project(p, half):
                b, u = divmod(p, 4)
                if half == 0:
                    if u == 0:
                        pe.wait_ge(s[f"w{b % 2}_in"], 16 * (b // 2 + 1))
                    if p >= 2:
                        pe.wait_ge(s["proj_out"], p - 1)
                w, ps = wbuf[b % 2], bank[p % 2]
                for dc in range(half * DC // 2, (half + 1) * DC // 2):
                    if p == 0:
                        pe.wait_ge(s["hT_rdy"], dc + 1)
                    if b < 3:
                        mm = pe.matmul(ps, w[:, dc, u * P:(u + 1) * P], hT[:, dc], start=dc == 0, stop=dc == DC - 1)
                    else:
                        mm = pe.matmul(ps, hT[:, dc, u * P:(u + 1) * P], w[:, dc], start=dc == 0, stop=dc == DC - 1)
                if half == 1:
                    mm.then_inc(s["proj_ps"], 1)

            def turn(kind, i):
                n = TR.index((kind, i, 0))
                if n >= 1:
                    pe.wait_ge(s["tr_out"], n)
                if kind == "fwd":
                    pe.wait_ge(s["silu_done"], i + 1)
                elif kind == "gback":
                    pe.wait_ge(s["gnorm"], NT * (i // GH + 1))
                else:
                    pe.wait_ge(s["snorm"], NT * (i // 4 + 1))
                for t in range(NT):
                    if kind == "fwd":
                        src = act_o[i % 2][:, t * P:(t + 1) * P]
                    elif kind == "gback":
                        src = tok["gk" if i < GH else "gq"][:, t, (i % GH) * GD:(i % GH + 1) * GD]
                    else:
                        src = tok["sq" if i < 4 else "sk"][:, t, (i % 4) * P:(i % 4 + 1) * P]
                    mm = pe.transpose(bank[2][:, t * P:(t + 1) * P], src, ident[:])
                mm.then_inc(s["tr_ps"], 1)

            def attention(kind, h, i):
                off, width, kbs = PARTS[i]
                n = 3 * h + i
                if kind == "z":
                    if n == 0:
                        pe.wait_ge(s["tr_out"], len(TR))
                        pe.wait_ge(s["proj_out"], NUNIT)
                    else:
                        pe.wait_ge(s["z_out"], n)
                    r = slice((h % 2) * SBD, (h % 2 + 1) * SBD)
                    for kb in kbs:
                        o = KB_OFF[kb] - off
                        mm = pe.matmul(bank[0][:, o:o + T - kb * P], skT[r, h // 2, kb * P:(kb + 1) * P],
                                       sqT[r, h // 2, kb * P:T], start=True, stop=True)
                    mm.then_inc(s["z_ps"], 1)
                elif kind == "r":
                    if i == 0:
                        pe.wait_ge(s["sp_rdy"], h + 1)
                    if n >= 1:
                        pe.wait_ge(s["arg_rdy"], n)
                    ops = []
                    for kb in kbs:
                        o = KB_OFF[kb] - off
                        ops.append((tri_ge, o, KB_OFF[kb], T - kb * P))
                        for k2 in range(kb + 1, NT):
                            ops.append((ones, o + (k2 - kb) * P, KB_OFF[k2], T - k2 * P))
                    for j, (m, o, src, w) in enumerate(ops):
                        mm = pe.matmul(bank[1][:, o:o + w], m[:], sp_[:, src:src + w], start=j == 0,
                                       stop=j == len(ops) - 1, skip_group_check=True)
                    mm.then_inc(s["r_ps"], 1)
                else:
                    pe.wait_ge(s["wt_rdy"], h + 1)
                    if h >= 1:
                        pe.wait_ge(s["o_out"], h)
                    for qt in range(NT):
                        for kb in range(qt + 1):
                            o = KB_OFF[kb] + (qt - kb) * P
                            mm = pe.matmul(bank[2][:, qt * SBD:(qt + 1) * SBD], wts[h % 2][:, o:o + P],
                                           tok["sv"][:, kb, h * SBD:(h + 1) * SBD], start=kb == 0, stop=kb == qt)
                    mm.then_inc(s["o_ps"], 1)

            for at_step, (kind, t, i) in enumerate(ORDER):
                n = t * NL + i
                if kind == "proj":
                    project(t, i)
                elif kind == "gate":
                    gate_steps(t)
                elif kind in ("fwd", "gback", "sback"):
                    turn(kind, t)
                elif kind in ("z", "r", "o"):
                    attention(kind, t, i)
                elif kind == "bc":
                    if t == 0:
                        pe.wait_ge(s["gate_dve"], 4)
                    else:
                        pe.wait_ge(s["ti_rdy"], 2 * NL * t)
                    for h in range(GH):
                        c = slice(h * P, (h + 1) * P)
                        pe.matmul(bank[4][:, c], g_[:, t, h:h + 1].to_broadcast([P, P]), tri_le[:], start=True, stop=True)
                        mm = pe.matmul(bank[5][:, c], beta[:, t, h:h + 1].to_broadcast([P, P]), ident[:],
                                       start=True, stop=True)
                    mm.then_inc(s["bc_ps"], 1)
                elif kind == "kk":
                    pe.wait_ge(s["kb_rdy"], t + 1)
                    for h in range(GH):
                        mm = pe.matmul(bank[6][:, h * P:(h + 1) * P], gkT[:, h, t * P:(t + 1) * P], kbT[:, h],
                                       start=True, stop=True)
                    mm.then_inc(s["kk_ps"], 1)
                elif kind == "qk":
                    if t == 0:
                        pe.wait_ge(s["tr_out"], TR.index(("gback", 7, 0)) + 1)
                    if count("os", at_step):
                        pe.wait_ge(s["s_rdy"], count("os", at_step) + 1)
                    if count("nw", at_step):
                        pe.wait_ge(s["nw_out"], count("nw", at_step))
                    for h in range(GH):
                        mm = pe.matmul(bank[7][:, h * P:(h + 1) * P], gkT[:, h, t * P:(t + 1) * P],
                                       gqT[:, h, t * P:(t + 1) * P], start=True, stop=True)
                    mm.then_inc(s["qk_ps"], 1)
                elif kind == "x":
                    pe.wait_ge(s["ats_rdy"], n + 1)
                    if i >= 1:
                        pe.wait_ge(s["ti_rdy"], 2 * n)
                    for h in range(GH):
                        mm = pe.matmul(bank[4][:, h * P:(h + 1) * P], ATs[n % 2][:, h], TI[:, h] if i else ident[:],
                                       start=True, stop=True)
                    mm.then_inc(s["x_ps"], 1)
                elif kind == "y" and i >= 1:
                    pe.wait_ge(s["x_out"], (NL - 1) * t + i)
                    for h in range(GH):
                        c = slice(h * P, (h + 1) * P)
                        tt = TTI[t % 2][:, h]
                        if i < NL - 1:
                            pe.matmul(bank[5][:, c], tt, XW[:, h], start=True, stop=True)
                        mm = pe.matmul(bank[6][:, c], XW[:, h], tt, start=True, stop=True)
                    mm.then_inc(s["y_ps"], 1)
                elif kind == "nw":
                    pe.wait_ge(s["ti_rdy"], 2 * NL * (t + 1))
                    pe.wait_ge(s["mul_rdy"], t + 1)
                    pe.wait_ge(s["attn_rdy"], count("qk", at_step))
                    pe.wait_ge(s["s_rdy"], t + 1)
                    for h in range(GH):
                        mm = pe.matmul(bank[7][:, h * P:(h + 1) * P], kbe[:, t, h * GD:(h + 1) * GD], TTI[t % 2][:, h],
                                       start=True, stop=True)
                    mm.then_inc(s["nw_ps"], 1)
                elif kind == "vn":
                    pe.wait_ge(s["nw_out"], t + 1)
                    if t >= 1:
                        pe.wait_ge(s["os_out"], t)
                    for h in range(GH):
                        c = slice(h * P, (h + 1) * P)
                        pe.matmul(bank[3][:, c], TTI[t % 2][:, h], vb[:, t, h * GD:(h + 1) * GD], start=True, stop=False)
                        mm = pe.matmul(bank[3][:, c], nv[:, h], S[:, h], start=False, stop=True)
                    mm.then_inc(s["vn_ps"], 1)
                elif kind == "os":
                    pe.wait_ge(s["vn_out"], t + 1)
                    pe.wait_ge(s["attn_rdy"], count("qk", at_step))
                    for h in range(GH):
                        c = slice(h * P, (h + 1) * P)
                        pe.matmul(bank[3][:, c], qdT[t % 2][:, h], S[:, h], start=True, stop=False)
                        pe.matmul(bank[3][:, c], attnT[t % 2][:, h], nv[:, h], start=False, stop=True)
                        mm = pe.matmul(bank[7][:, c], kd[:, h * GD:(h + 1) * GD], nv[:, h], start=True, stop=True)
                    mm.then_inc(s["os_ps"], 1)

            def turn_mix(t):
                if t <= 1:
                    pe.wait_ge(s["mix_rdy"], 3 if t else 1)
                else:
                    pe.wait_ge(s["mixT_out"], t - 1)
                for c in range(DC):
                    src = osb[:, t, c * P:(c + 1) * P] if c < 4 else og[:, t, (c - 4) * P:(c - 3) * P]
                    mm = pe.transpose(bank[2 * (t % 2) + c // 4][:, (c % 4) * P:(c % 4 + 1) * P], src, ident[:])
                mm.then_inc(s["mixT_ps"], 1)

            def mix_out(n):
                t, half = divmod(n, 2)
                pe.wait_ge(s["mixT_out"], t + 1)
                if n >= 4:
                    pe.wait_ge(s["x2_rdy"], n - 1)
                for c in range(DC):
                    mm = pe.matmul(bank[wo_bank(n)], mixT[:, t, c], w_out_s[c][:, half * 512:(half + 1) * 512],
                                   start=c == 0, stop=c == DC - 1)
                mm.then_inc(s["wo_ps"], 1)

            turn_mix(0)
            pe.wait_ge(s["wout_in"], 16 * DC)
            mix_out(0)
            mix_out(1)
            for t in range(1, NT):
                turn_mix(t)
            mix_out(2)
            pe.wait_ge(s["mixT_out"], NT)
            def turn_h2(t):
                pe.wait_ge(s["h2_rdy"], t + 1)
                for c in range(DC):
                    mm = pe.transpose(bank[c // 4][:, (c % 4) * P:(c % 4 + 1) * P], h2[:, c * P:(c + 1) * P], ident[:])
                mm.then_inc(s["h2T_ps"], 1)

            def query(j, part, parts):
                for c in range(part * DC // parts, (part + 1) * DC // parts):
                    mm = pe.matmul(bank[j // 4][:, (j % 4) * P:(j % 4 + 1) * P], w_q_s[c][:, j * HALF:(j + 1) * HALF],
                                   h2T[:, c], start=c == 0, stop=c == DC - 1)
                return mm

            def scores(t, j0=0, j1=NS):
                pe.wait_ge(s["q_out"], t + (2 if j1 == NS else 1))
                for j in range(j0, j1):
                    mm = pe.matmul(bank[j // 4][:, (j % 4) * NKEYS:(j % 4 + 1) * NKEYS], qs[:, j], keysT[:, j],
                                   start=True, stop=True)
                mm.then_inc(s["sc_ps"], 1)

            turn_h2(0)
            pe.wait_ge(s["wq_in"], 16 * DC)
            pe.wait_ge(s["h2T_out"], 1)
            for j in range(NS):
                if j == 2 * AHEAD + 1:
                    pe.wait_ge(s["keys_in"], 16)
                    scores(0, 0, 2 * AHEAD)
                mm = query(j, 0, 1)
                if j in (2 * AHEAD - 1, NS - 1):
                    mm.then_inc(s["q_ps"], 1)
            scores(0, 2 * AHEAD)
            for n in range(3, 2 * NT):
                mix_out(n)
            x2 = xs.rearrange("p t d -> p (t d)")

            def tile(i):
                pe.wait_ge(s["y_out"], i + 1)
                if is_first(i):
                    pe.wait_ge(s["x2_rdy"], 2 * NT)
                for half in range(2):
                    pe.matmul(bank[6 + half], ident[:], x2[:, bass.ds(i * D + half * 512, 512)], start=True,
                              stop=False, skip_group_check=True)
                for c in range(SEL):
                    if not is_last(i):
                        if c == TURN_AT:
                            pe.wait_ge(s["picked"], (i + 1) * PH)
                            turn_h2(i + 1)
                        if QUERY_AT <= c < SCORE_AT:
                            if c == QUERY_AT:
                                pe.wait_ge(s["h2T_out"], i + 2)
                            mm = query((c - QUERY_AT) // 2, (c - QUERY_AT) % 2, 2)
                            if c == SCORE_AT - 1:
                                mm.then_inc(s["q_ps"], 1)
                        if c == SCORE_AT:
                            scores(i + 1)
                    pe.wait_ge(s["diag_rdy"], i * SEL + c + 1)
                    pe.wait_ge(v_in[c % VB], 16 * (i * (SEL // VB) + c // VB + 1))
                    for half in range(2):
                        mm = pe.matmul(bank[6 + half], diag[c % VB], v_row[c % VB][:, half * 512:(half + 1) * 512],
                                       start=False, stop=c == SEL - 1, skip_group_check=True)
                    mm.then_inc(s["v_free"], 1)

            tiles(pe, tile)

        @block.scalar
        def _(act):
            act.wait_ge(s["x_scale"], 1)
            for t in range(NT // 2):
                act.activation(xn[:, t], xs[:, t], ACT.Copy, scale=st[:, 0, t:t + 1]).then_inc(s["xn_rdy"], 1)
            act.wait_ge(s["par_in"], 16 * NPAR)
            for dc in range(DC):
                act.wait_ge(s["xT_ps"], dc + 1)
                act.activation(hT[:, dc], bank[4 + dc % 2], ACT.Copy, scale=g1c[:, dc:dc + 1]).then_inc(s["hT_rdy"], 1)

            def gate_steps(step):
                if step == 0:
                    act.wait_ge(s["ab_ps"], 1)
                    act.copy(abT, bank[7][0:2 * GH]).then_inc(s["ab_rdy"], 1)
                elif step == 1:
                    act.preload_act_table_set("natural_log_exp_and_others")
                    act.activation(st[:, 3, 4 * GH:5 * GH], abc[:, 0:GH], ACT.Exp).then_inc(s["gate_act"], 1)
                    act.wait_ge(s["gate_dve"], 1)
                    act.activation(gt2, gt2, ACT.Exp)
                    act.activation(gt3, ab[:, :, GH:], ACT.Exp, scale=-1.0)
                    act.drain()
                    act.activation(gt2, gt2, ACT.Ln, bias=1.0).then_inc(s["gate_act"], 1)
                elif step == 3:
                    act.wait_ge(s["gate_ps"], 1)
                    sums = bank[3][:, 0:48].rearrange("p (a t h) -> p a t h", a=3, t=NT)
                    act.mul(ngc, sums[:, 0], -1.0)
                    act.activation(egc, sums[:, 0], ACT.Exp)
                    act.activation(ekd, sums[:, 1], ACT.Exp)
                    act.activation(etot, sums[:, 2], ACT.Exp).then_inc(s["gate_act"], 1)

            def projected(p):
                b, u = divmod(p, 4)
                act.wait_ge(s["proj_ps"], p + 1)
                if b < 3:
                    act.wait_ge(s["raw_clear"], 1)
                    if p >= 2:
                        act.wait_ge(s["conv_done"], p - 1)
                    act.copy(raw[p % 2][:, CONV - 1:], bank[p % 2]).then_inc(s["proj_out"], 1)
                elif BLOCKS[b] == "z":
                    act.activation(tok["z"][:, u], bank[p % 2], ACT.Silu).then_inc(s["proj_out"], 1)
                    if u == 3:
                        act.preload_act_table_set("natural_log_exp_and_others")
                else:
                    act.copy(tok[BLOCKS[b]][:, u], bank[p % 2]).then_inc(s["proj_out"], 1)
                if 1 <= p <= 12:
                    j = p - 1
                    act.wait_ge(s["conv_done"], j + 1)
                    if j >= 2:
                        act.wait_ge(s["tr_ps"], TR.index(("fwd", j - 2, 0)) + 1)
                    act.activation(act_o[j % 2], conv[j % 2], ACT.Silu).then_inc(s["silu_done"], 1)
                if p in NORM_AT:
                    j = NORM_AT.index(p)
                    act.drain()
                    if j:
                        act.wait_ge(s["rs_rdy"], j)
                    act.activation(squares, tok[BLOCKS[j]].rearrange("p t d -> p (t d)"), ACT.Square).then_inc(s["sq_rdy"], 1)

            def turned(kind, i):
                n = TR.index((kind, i, 0))
                act.wait_ge(s["tr_ps"], n + 1)
                if kind == "fwd":
                    h = i % GH
                    dst = tok[BLOCKS[i // GH]][:, :, h * GD:(h + 1) * GD]
                    ins = act.copy(dst, bank[2].rearrange("p (t d) -> p t d", t=NT))
                elif kind == "gback":
                    ins = act.copy((gkT if i < GH else gqT)[:, i % GH], bank[2])
                else:
                    ins = act.activation((sqT if i < 4 else skT)[:, i % 4], bank[2], ACT.Copy,
                                         scale=sgc[:, i // 4:i // 4 + 1])
                ins.then_inc(s["tr_out"], 1)

            for kind, t, i in ORDER:
                n = t * NL + i
                if kind == "proj":
                    if i == 1:
                        projected(t)
                elif kind == "gate":
                    gate_steps(t)
                elif kind in ("fwd", "gback", "sback"):
                    turned(kind, t)
                elif kind == "z" and i == 2:
                    h = t
                    act.wait_ge(s["nabs_rdy"], h + 1)
                    act.activation(ez, ez, ACT.Exp).then_inc(s["e_rdy"], 1)
                    act.wait_ge(s["e_rdy"], h + 1)
                    act.activation(ez, ez, ACT.Ln, bias=1.0).then_inc(s["l_rdy"], 1)
                elif kind == "r" and i == 2:
                    h = t
                    act.wait_ge(s["arg_rdy"], 3 * h + 3)
                    if h >= 2:
                        act.wait_ge(s["o_ps"], h - 1)
                    act.activation(wts[h % 2], zs[h % 2], ACT.Exp).then_inc(s["wt_rdy"], 1)
                elif kind == "o":
                    h = t
                    act.wait_ge(s["o_ps"], h + 1)
                    act.copy(osb[:, :, h * SBD:(h + 1) * SBD],
                             bank[2][:, 0:NT * SBD].rearrange("p (t d) -> p t d", t=NT)).then_inc(s["o_out"], 1)
                elif kind == "bc":
                    act.wait_ge(s["bc_ps"], t + 1)
                    if t == 0:
                        act.wait_ge(s["raw_free"], 1)
                    if t >= 2:
                        act.wait_ge(s["os_ps"], t - 1)
                    act.activation(qdT[t % 2], heads(bank[4]), ACT.Exp).then_inc(s["qd_rdy"], 1)
                    act.wait_ge(s["arg_g"], t + 1)
                    for h in range(GH):
                        ins = act.activation(decT[:, h], decT[:, h], ACT.Exp, bias=ngc[:, t, h:h + 1])
                    ins.then_inc(s["dec_rdy"], 1)
                elif kind == "x" and i >= 1:
                    act.wait_ge(s["x_ps"], n + 1)
                    act.copy(XW, heads(bank[4])).then_inc(s["x_out"], 1)
                elif kind == "nw":
                    act.wait_ge(s["nw_ps"], t + 1)
                    if t >= 1:
                        act.wait_ge(s["os_ps"], t)
                    act.copy(nv, heads(bank[7])).then_inc(s["nw_out"], 1)
                elif kind == "vn":
                    act.wait_ge(s["vn_ps"], t + 1)
                    act.copy(nv, heads(bank[3])).then_inc(s["vn_out"], 1)
                elif kind == "os":
                    act.wait_ge(s["os_ps"], t + 1)
                    act.copy(og[:, t], bank[3]).then_inc(s["os_out"], 1)

            for t in range(NT):
                act.wait_ge(s["mixT_ps"], t + 1)
                for a, gain in enumerate((sgc[:, 2:3], ggc[:])):
                    ins = act.activation(mixT[:, t, 4 * a:4 * a + 4], bank[2 * (t % 2) + a].rearrange("p (c i) -> p c i", c=4),
                                         ACT.Copy, scale=gain)
                ins.then_inc(s["mixT_out"], 1)

            def turned_h2(t):
                act.wait_ge(s["h2T_ps"], t + 1)
                act.copy(h2T, psum[:, 0:2].rearrange("p a (b i) -> p (a b) i", i=P)).then_inc(s["h2T_out"], 1)

            def queries(t, j0=0, j1=NS):
                act.wait_ge(s["q_ps"], t + (2 if j1 == NS else 1))
                act.copy(qs[:, j0:j1], psum[:, 0:4].rearrange("p a (b i) -> p (a b) i", i=P)[:, j0:j1]).then_inc(s["q_out"], 1)

            def soft(group, where, h0, h1):
                c = slice(h0 * TOPK, h1 * TOPK)
                act.wait_ge(s["best_rdy"], group + 1)
                act.activation(where[:, c], where[:, c], ACT.Exp).then_inc(s["e_out"], 1)

            def diagonal(row, c):
                act.wait_ge(s["v_free"], SEL + row + c - VB + 1)
                act.activation(diag[c % VB], ident[:], ACT.Copy, scale=wt[:, c:c + 1]).then_inc(s["diag_rdy"], 1)

            def finish(i):
                act.wait_ge(s["w_rdy"], i * PH + PH)
                for c in range((PH - 1) * TOPK, SEL):
                    diagonal(i * SEL, c)
                act.wait_ge(s["v_free"], SEL + i * SEL + SEL)
                act.wait_ge(s["stored"], 16 * (i + 1))
                for half in range(2):
                    ins = act.copy(y_s[:, half * 512:(half + 1) * 512], bank[6 + half])
                ins.then_inc(s["y_out"], 1)

            def load_h2(i):
                act.wait_ge(s["u_free"], i * SEL + UB)
                for half in range(2):
                    ins = act.copy(bank[4 + half], h2[:, half * 512:(half + 1) * 512])
                ins.then_inc(s["h2p_rdy"], 1)

            turned_h2(0)
            queries(0, 0, 2 * AHEAD)
            load_h2(0)
            soft(0, gates, 0, EARLY)
            queries(0, 2 * AHEAD)

            def tile(i):
                if not is_first(i):
                    load_h2(i)
                def gelu(h):
                    c = slice(h * TOPK, (h + 1) * TOPK)
                    act.wait_ge(s["dots_rdy"], i * PH + h + 1)
                    act.activation(gel[:, c], dots[:, c], ACT.Gelu).then_inc(s["gel_rdy"], 1)

                for h in range(PH):
                    if is_first(i) and h == 1:
                        soft(1, gates, *GROUPS0[1][:2])
                        gelu(1)
                        act.wait_ge(s["wo_ps"], 2 * NT)
                    if h >= 1:
                        act.wait_ge(s["w_rdy"], i * PH + h)
                        for c in range((h - 1) * TOPK, h * TOPK):
                            if c == TURN_AT and not is_last(i):
                                turned_h2(i + 1)
                            if c == SCORE_AT and not is_last(i):
                                queries(i + 1)
                            if c == EXP_AT and not is_last(i):
                                soft(len(GROUPS0) + i, gates_n, 0, PH)
                            if is_first(i) and c == GROUPS0[2][2]:
                                soft(2, gates, *GROUPS0[2][:2])
                            diagonal(i * SEL, c)
                    elif not is_first(i):
                        finish(i - 1)
                    if not (is_first(i) and h == 1):
                        gelu(h)

            tiles(act, tile)
            finish(NT - 1)

        @block.vector
        def _(dve):
            def rsqrt(dst, v, n, add):
                t = st[:, 2, 0:dst.shape[-1]]
                w = st[:, 1, 0:dst.shape[-1]]
                dve.tensor_scalar(w, v, n, add, ALU.mult, ALU.add)
                dve.drain()
                dve.tensor_scalar(dst.bitcast(I32), w.bitcast(I32), 1, None, ALU.arith_shift_right)
                dve.drain()
                dve.tensor_scalar(dst.bitcast(I32), dst.bitcast(I32), -1.0, float(0x5F3759DF), ALU.mult, ALU.add)
                dve.drain()
                for _ in range(3):
                    dve.tensor_tensor(t, dst, dst, ALU.mult)
                    dve.drain()
                    dve.scalar_tensor_tensor(t, t, -0.5, w, ALU.mult, ALU.mult)
                    dve.drain()
                    dve.scalar_tensor_tensor(dst, t, 1.5, dst, ALU.add, ALU.mult)
                    dve.drain()

            def norm_rows(v, heads_, width, n, add, extra, tmp):
                k = v.shape[1] * heads_
                vv = v.rearrange("p t (h d) -> p (t h) d", h=heads_)
                sv = tmp[:, 0:k * width].rearrange("p (k d) -> p k d", k=k)
                dve.drain()
                dve.tensor_tensor(sv, vv, vv, ALU.mult)
                dve.drain()
                ss, rs = st[:, 3, 0:k], st[:, 0, 0:k]
                dve.tensor_reduce(ss, sv, AX.X, ALU.add)
                dve.drain()
                rsqrt(rs, ss, n, add)
                if extra != 1.0:
                    dve.tensor_scalar(rs, rs, extra, None, ALU.mult)
                    dve.drain()
                return dve.tensor_tensor(vv, vv, rs.unsqueeze(2).to_broadcast([P, k, width]), ALU.mult)

            for t in range(NT):
                dve.wait_ge(s[f"x{t}_in"], 16)
                dve.tensor_tensor_reduce(xn[:, t], xs[:, t], xs[:, t], 1.0, 0.0, ALU.mult, ALU.add, st[:, 3, t:t + 1])
            dve.drain()
            rsqrt(st[:, 0, 0:NT], st[:, 3, 0:NT], 1.0 / D, EPS)
            dve.engine_nop().then_inc(s["x_scale"], 1)
            for t in range(NT // 2, NT):
                dve.tensor_scalar(xn[:, t], xs[:, t], st[:, 0, t:t + 1], None, ALU.mult).then_inc(s["xn_rdy"], 1)

            dve.wait_ge(s["xT_ps"], DC)
            for rr in raw:
                ins = dve.memset(rr[:, 0:CONV - 1], 0.0)
            ins.then_inc(s["raw_clear"], 1)

            def conv_unit(i):
                dve.wait_ge(s["proj_out"], i + 1)
                if i >= 2:
                    dve.wait_ge(s["silu_done"], i - 1)
                b, h = divmod(i, GH)
                r, c, w = raw[i % 2], conv[i % 2], cwc[:, ("gq", "gk", "gv").index(BLOCKS[b]) * GH + h]
                dve.tensor_scalar(c, r[:, 0:T], w[:, 0:1], None, ALU.mult)
                for j in range(1, CONV):
                    dve.drain()
                    ins = dve.scalar_tensor_tensor(c, r[:, j:j + T], w[:, j:j + 1], c, ALU.mult, ALU.add)
                ins.then_inc(s["conv_done"], 1)

            def gate_steps(step):
                if step == 1:
                    dve.wait_ge(s["ab_ps"], 2)
                    dve.wait_ge(s["par_in"], 16 * NPAR)
                    dve.tensor_copy(ab[:], bank[7][:, 0:NT * 2 * GH].rearrange("p (t c) -> p t c", t=NT))
                    dve.drain()
                    dve.tensor_tensor(gt1, ab[:, :, 0:GH], abc[:, GH:].unsqueeze(1).to_broadcast([P, NT, GH]), ALU.add)
                    dve.drain()
                    dve.scalar_tensor_tensor(gt2, gt1, -1.0, gt1, ALU.mult, ALU.min).then_inc(s["gate_dve"], 1)
                elif step == 2:
                    dve.wait_ge(s["gate_act"], 2)
                    dve.drain()
                    dve.scalar_tensor_tensor(gt1, gt1, 0.0, gt2, ALU.max, ALU.add)
                    dve.tensor_scalar(gt3, gt3, 1.0, None, ALU.add)
                    nea = st[:, 3, 5 * GH:6 * GH]
                    dve.tensor_scalar(nea, st[:, 3, 4 * GH:5 * GH], -1.0, None, ALU.mult)
                    dve.drain()
                    dve.reciprocal(beta, gt3)
                    dve.tensor_tensor(g_, gt1, nea.unsqueeze(1).to_broadcast([P, NT, GH]), ALU.mult).then_inc(s["gate_dve"], 1)
                elif step == 4:
                    dve.wait_ge(s["gate_act"], 3)
                    dve.drain()
                    dve.scalar_tensor_tensor(nbe, egc, -1.0, beta, ALU.mult, ALU.mult).then_inc(s["gate_dve"], 1)
                    dve.drain()
                    dve.engine_nop().then_inc(s["gate_dve"], 1)

            def softplus_head(h):
                dve.wait_ge(s["l_rdy"], h + 1)
                if h >= 1:
                    dve.wait_ge(s["r_ps"], 3 * h)
                dve.scalar_tensor_tensor(sp_, zs[h % 2], 0.0, ez, ALU.max, ALU.add).then_inc(s["sp_rdy"], 1)

            def projected(p):
                if p < 3 * GH:
                    conv_unit(p)
                if p in NORM_AT:
                    j = NORM_AT.index(p)
                    ss, rs = st[:, 3, 0:NT * GH], g_rs[:, j]
                    dve.wait_ge(s["sq_rdy"], j + 1)
                    dve.drain()
                    dve.tensor_reduce(ss, squares.rearrange("p (k d) -> p k d", d=GD), AX.X, ALU.add)
                    dve.drain()
                    rsqrt(rs, ss, 1.0, EPS)
                    if j:
                        dve.tensor_scalar(rs, rs, GD ** -0.5, None, ALU.mult)
                        dve.drain()
                    dve.engine_nop().then_inc(s["rs_rdy"], 1)
                b, u = divmod(p, 4)
                if BLOCKS[b] in ("sq", "sk"):
                    dve.wait_ge(s["proj_out"], p + 1)
                    norm_rows(tok[BLOCKS[b]][:, u:u + 1], SBH, SBD, 1.0 / SBD, EPS, SBD ** -0.5 if BLOCKS[b] == "sq" else 1.0,
                              squares).then_inc(s["snorm"], 1)

            def out_norm(t):
                dve.wait_ge(s["os_out"], t + 1)
                norm_rows(og[:, t:t + 1], GH, GD, 1.0 / GD, EPS, 1.0, squares_b)
                dve.drain()
                return dve.tensor_tensor(og[:, t], og[:, t], tok["z"][:, t], ALU.mult)

            for kind, t, i in ORDER:
                n = t * NL + i
                if kind == "proj" and i == 1:
                    projected(t)
                elif kind == "gate":
                    gate_steps(t)
                elif kind == "fwd" and t == 3 * GH - 1:
                    dve.wait_ge(s["tr_ps"], TR.index(("fwd", t, 0)) + 1)
                    dve.memset(S, 0.0).then_inc(s["s_rdy"], 1)
                    dve.engine_nop().then_inc(s["raw_free"], 1)
                elif kind == "z":
                    h, m = t, 3 * t + i
                    off, width, _ = PARTS[i]
                    dve.wait_ge(s["z_ps"], m + 1)
                    if i == 0 and h >= 2:
                        dve.wait_ge(s["wt_rdy"], h - 1)
                    dve.tensor_tensor(zs[h % 2][:, off:off + width], bank[0][:, 0:width],
                                      sb_mask[:, off:off + width], ALU.add).then_inc(s["z_out"], 1)
                    if i == 2:
                        dve.drain()
                        dve.scalar_tensor_tensor(ez, zs[h % 2], -1.0, zs[h % 2], ALU.mult, ALU.min).then_inc(s["nabs_rdy"], 1)
                        if h == 0:
                            softplus_head(0)
                elif kind == "r":
                    h, m = t, 3 * t + i
                    off, width, _ = PARTS[i]
                    dve.wait_ge(s["r_ps"], m + 1)
                    z = zs[h % 2][:, off:off + width]
                    dve.tensor_tensor(z, z, bank[1][:, 0:width], ALU.subtract).then_inc(s["arg_rdy"], 1)
                    if i == 2 and h + 1 < SBH:
                        softplus_head(h + 1)
                elif kind == "bc":
                    dve.wait_ge(s["qd_rdy"], t + 1)
                    dve.drain()
                    dve.tensor_tensor(decT, heads(bank[4]), causal_add[:].unsqueeze(1).to_broadcast([P, GH, P]), ALU.add).then_inc(s["arg_g"], 1)
                    dve.wait_ge(s["tr_out"], TR.index(("gback", 3, 0)) + 1)
                    dve.tensor_tensor(kbT, gkT[:, :, t * P:(t + 1) * P], heads(bank[5]), ALU.mult).then_inc(s["kb_rdy"], 1)
                elif kind == "kk":
                    dve.wait_ge(s["kk_ps"], t + 1)
                    dve.wait_ge(s["dec_rdy"], t + 1)
                    if t >= 1:
                        dve.wait_ge(s["ats_rdy"], NL * t)
                    dve.tensor_tensor(AT, heads(bank[6]), decT, ALU.mult).then_inc(s["at_rdy"], 1)
                elif kind == "qk":
                    dve.wait_ge(s["qk_ps"], t + 1)
                    if t >= 2:
                        dve.wait_ge(s["os_ps"], t - 1)
                    dve.tensor_tensor(qdT[t % 2], qdT[t % 2], gqT[:, :, t * P:(t + 1) * P], ALU.mult)
                    dve.tensor_tensor(attnT[t % 2], heads(bank[7]), decT, ALU.mult)
                    dve.drain()
                    dve.engine_nop().then_inc(s["attn_rdy"], 1)
                elif kind == "y":
                    tt = TTI[t % 2]
                    if i == 0:
                        idb = ident[:].unsqueeze(1).to_broadcast([P, GH, P])
                        dve.wait_ge(s["x_ps"], n + 1)
                        if t >= 2:
                            dve.wait_ge(s["vn_ps"], t - 1)
                        dve.drain()
                        dve.tensor_tensor(TI, idb, heads(bank[4]), ALU.subtract).then_inc(s["ti_rdy"], 1)
                        dve.tensor_tensor(tt, idb, ATs[n % 2], ALU.subtract).then_inc(s["ti_rdy"], 1)
                    else:
                        dve.wait_ge(s["y_ps"], (NL - 1) * t + i)
                        dve.drain()
                        if i < NL - 1:
                            dve.tensor_tensor(TI, TI, heads(bank[5]), ALU.subtract).then_inc(s["ti_rdy"], 1)
                        else:
                            dve.engine_nop().then_inc(s["ti_rdy"], 1)
                        dve.tensor_tensor(tt, tt, heads(bank[6]), ALU.subtract).then_inc(s["ti_rdy"], 1)
                elif kind == "nw" and t >= 1:
                    out_norm(t - 1)
                elif kind == "os":
                    dve.wait_ge(s["os_ps"], t + 1)
                    dve.drain()
                    dve.tensor_tensor(S, S, etot[:, t].unsqueeze(2).to_broadcast([P, GH, P]), ALU.mult)
                    dve.drain()
                    dve.tensor_tensor(S, S, heads(bank[7]), ALU.add).then_inc(s["s_rdy"], 1)

            dve.wait_ge(s["o_out"], SBH)
            norm_rows(osb[:, 0:1], SBH, SBD, 1.0 / SBD, EPS, 1.0, squares_b).then_inc(s["mix_rdy"], 1)
            out_norm(NT - 1).then_inc(s["mix_rdy"], 1)
            norm_rows(osb[:, 1:], SBH, SBD, 1.0 / SBD, EPS, 1.0, squares_c).then_inc(s["mix_rdy"], 1)

            def residual(n):
                t, half = divmod(n, 2)
                dve.wait_ge(s["wo_ps"], n + 1)
                xv = xs[:, t, half * 512:(half + 1) * 512]
                dve.tensor_tensor(xv, xv, bank[wo_bank(n)], ALU.add).then_inc(s["x2_rdy"], 1)

            residual(0)
            residual(1)

            dve.engine_nop().then_inc(s["u_free"], UB)
            dve.engine_nop().then_inc(s["v_free"], SEL)
            dve.engine_nop().then_inc(s["y_out"], 1)
            dve.engine_nop().then_inc(s["stored"], 16)
            idb16 = iota[:].unsqueeze(1).to_broadcast([P, TOPK, TOPK])

            def top16(out, idx, vals, left):
                for o, i_, v, l_ in zip(out, idx, vals, left):
                    dve.max(o[:, 0:8], v)
                dve.drain()
                for o, i_, v, l_ in zip(out, idx, vals, left):
                    dve.max_index(i_[:, 0:8], o[:, 0:8], v)
                    dve.match_replace(l_, o[:, 0:8], v, LOWEST)
                dve.drain()
                for o, i_, v, l_ in zip(out, idx, vals, left):
                    dve.max(o[:, 8:16], l_)
                dve.drain()
                for o, i_, v, l_ in zip(out, idx, vals, left):
                    ins = dve.max_index(i_[:, 8:16], o[:, 8:16], l_)
                return ins

            def norm2(t):
                xt = x2[:, bass.ds(t * D, D)]
                if not is_first(t):
                    by_itself(dve, s["h2T_ps"], t)
                dve.drain()
                dve.tensor_tensor(h2sq, xt, xt, ALU.mult)
                dve.drain()
                dve.tensor_reduce(st[:, 3, 0:1], h2sq, AX.X, ALU.add)
                dve.drain()
                rsqrt(st[:, 0, 0:1], st[:, 3, 0:1], 1.0 / D, EPS)
                dve.scalar_tensor_tensor(h2, xt, st[:, 0, 0:1], g2b, ALU.mult, ALU.mult).then_inc(s["h2_rdy"], 1)

            def choose(t, h, into_id, into_gate, signal):
                c = slice(h * TOPK, (h + 1) * TOPK)
                by_itself(dve, s["sc_ps"], t + (1 if is_first(t) and h < AHEAD else 2))
                dve.drain()
                sc_ = [bank[(2 * h + a) // 4][:, ((2 * h + a) % 4) * NKEYS:((2 * h + a) % 4 + 1) * NKEYS] for a in range(2)]
                top16([top[:, 0], top[:, 1]], [topi[:, 0], topi[:, 1]], sc_, [rest[:, 0], rest[:, 1]])
                dve.drain()
                dve.engine_nop().then_inc(s["picked"], 1)
                dve.tensor_tensor(cand.rearrange("p (a b) -> p a b", a=TOPK), top[:, 0].unsqueeze(2).to_broadcast([P, TOPK, TOPK]),
                                  top[:, 1].unsqueeze(1).to_broadcast([P, TOPK, TOPK]), ALU.add)
                dve.drain()
                top16([best], [pos], [cand], [crest])
                dve.drain()
                ins = dve.tensor_scalar(into_gate[:, c], best, best[:, 0:1], None, ALU.subtract)
                if signal:
                    ins.then_inc(s["best_rdy"], 1)
                dve.tensor_scalar(pos1, pos, 4, None, ALU.logical_shift_right)
                dve.tensor_scalar(pos2, pos, TOPK - 1, None, ALU.bitwise_and)
                dve.drain()
                for e, q in ((eq1, pos1), (eq2, pos2)):
                    dve.tensor_tensor(e, q.unsqueeze(2).to_broadcast([P, TOPK, TOPK]), idb16, ALU.is_equal)
                dve.drain()
                for e, a in ((eq1, 0), (eq2, 1)):
                    dve.tensor_tensor(e, e, topi[:, a].unsqueeze(1).to_broadcast([P, TOPK, TOPK]), ALU.mult)
                dve.drain()
                dve.tensor_reduce(id1, eq1, AX.X, ALU.add)
                dve.tensor_reduce(id2, eq2, AX.X, ALU.add)
                dve.drain()
                ins = dve.scalar_tensor_tensor(into_id[:, c], id1, float(NKEYS), id2, ALU.mult, ALU.add)
                if is_first(t):
                    ins.then_inc(s["eid_rdy"], 1)

            def soften(group, src, h0, h1):
                k = h1 - h0
                c = slice(h0 * TOPK, h1 * TOPK)
                src, dst = (v[:, c].rearrange("p (h k) -> p h k", h=k) for v in (src, gates))
                by_itself(dve, s["e_out"], group + 1)
                dve.tensor_reduce(esum[:, 0:k], src, AX.X, ALU.add)
                dve.drain()
                dve.reciprocal(erec[:, 0:k], esum[:, 0:k])
                dve.drain()
                dve.tensor_tensor(dst, src, erec[:, 0:k].unsqueeze(2).to_broadcast([P, k, TOPK]), ALU.mult)

            def take(h0, h1):
                c = slice(h0 * TOPK, h1 * TOPK)
                dve.drain()
                dve.tensor_copy(eid[:, c], eid_n[:, c]).then_inc(s["eid_rdy"], h1 - h0)

            x2 = xs.rearrange("p t d -> p (t d)")
            dve.wait_ge(s["g2_in"], 16)
            norm2(0)
            residual(2)
            for h in range(EARLY):
                choose(0, h, eid, gates, h == EARLY - 1)
            soften(0, gates, 0, EARLY)

            def tile(i):
                for h in range(PH):
                    if h == 0:
                        dve.wait_ge(s["h2p_rdy"], i + 1)
                    for k in range(TOPK):
                        c = h * TOPK + k
                        if is_first(i) and c in RESIDUAL_AT:
                            residual(3 + RESIDUAL_AT.index(c))
                        by_itself(dve, u_in[c % UB], 16 * (i * (SEL // UB) + c // UB + 1))
                        dve.tensor_tensor_reduce(u_row[c % UB], u_row[c % UB], h2p, 1.0, 0.0, ALU.mult, ALU.add,
                                                 dots[:, c:c + 1]).then_inc(s["u_free"], 1)
                        if c == TAKE_AT and not is_last(i):
                            by_itself(dve, s["v_free"], SEL + i * SEL + (PH - 2) * TOPK)
                            take(0, PH - 2)
                        if chosen_after(i, c):
                            who, head = chosen_after(i, c)
                            last = head in ([PH - 1] if who else [h1 - 1 for _, h1, _, _ in GROUPS0])
                            choose(i + who, head, *((eid_n, gates_n) if who else (eid, gates)), last)
                    dve.drain()
                    dve.engine_nop().then_inc(s["dots_rdy"], 1)
                    for group, (h0, h1, _, before) in enumerate(GROUPS0):
                        if is_first(i) and h == before:
                            soften(group, gates, h0, h1)
                    if h == 0 and not is_first(i):
                        soften(len(GROUPS0) + i - 1, gates_n, 0, PH)
                    c = slice(h * TOPK, (h + 1) * TOPK)
                    by_itself(dve, s["gel_rdy"], i * PH + h + 1)
                    dve.drain()
                    dve.tensor_tensor(wt[:, c], gel[:, c], gates[:, c], ALU.mult).then_inc(s["w_rdy"], 1)
                    if h == 1 and not is_first(i):
                        by_itself(dve, s["v_free"], SEL + i * SEL)
                        take(PH - 2, PH)
                    if h == 2 and not is_last(i):
                        norm2(i + 1)

            tiles(dve, tile)



_OUTS = ((1, T, D), "float32")


def kernel(**inputs):
    import numpy as _np
    import concourse.bacc as _bacc
    from concourse import mybir as _mybir
    from concourse.bass_utils import run_bass_kernel_spmd as _run

    a = {k: _np.asarray(v) for k, v in inputs.items()}
    a["norm1_g"] = a["norm1_g"][0].reshape(DC, P).T
    a["gdn_conv_w"] = a["gdn_conv_w"][0].reshape(CONV, 3 * GH, P).transpose(2, 1, 0)
    keys = _np.stack([a.pop("peer_keys1")[0], a.pop("peer_keys2")[0]], 1)
    a["keys_t"] = keys.reshape(1, NS, NKEYS, HALF).transpose(0, 1, 3, 2)

    nc = _bacc.Bacc("TRN2", target_bir_lowering=False, num_devices=1)
    arrays, args = {}, []
    for name in ("x", "norm1_g", "w_in", "sb_q_norm_g", "sb_k_norm_g", "sb_out_norm_g", "gdn_conv_w", "gdn_a_log",
                 "gdn_dt_bias", "gdn_out_norm_g", "w_out", "norm2_g", "peer_w_q", "keys_t", "peer_u", "peer_v"):
        v = _np.ascontiguousarray(a[name])
        arrays[f"in_{name}"] = v
        args.append(nc.dram_tensor(f"in_{name}", v.shape, _mybir.dt.from_np(v.dtype), kind="ExternalInput").ap())
    out = nc.dram_tensor("out_0", _OUTS[0], _mybir.dt.from_np(_np.dtype(_OUTS[1])), kind="ExternalOutput").ap()
    layer_kernel(nc, *args, out)
    r = _run(nc, [arrays], core_ids=[0])
    return r.results[0]["out_0"]
```
